# Optimizing a Trainium2 kernel written in Bass

```python
import jax, jax.numpy as jnp
from jax import lax
import numpy as np

D_MODEL = 1024
BATCH = 1
SEQ = 1024
DEPTH = 1

CHUNK = 64
Q_BLOCK = 128
EPS = 1e-6

SB_HEADS = 8
SB_HEAD_DIM = 64
SB_WIDTH = SB_HEADS * SB_HEAD_DIM

DF_HEADS = 4
DF_HEAD_DIM = 64
DF_V_DIM = 2 * DF_HEAD_DIM
DF_WIDTH = DF_HEADS * DF_V_DIM
DF_QK_WIDTH = DF_HEADS * 2 * DF_HEAD_DIM

N_BRANCH = 2
IN_SIZES = (SB_WIDTH, SB_WIDTH, SB_WIDTH, SB_WIDTH,
            DF_QK_WIDTH, DF_QK_WIDTH, DF_WIDTH, DF_WIDTH)
IN_COLS = sum(IN_SIZES)
IN_SPLITS = tuple(int(v) for v in np.cumsum(IN_SIZES)[:-1])

kernel_name = "hybrid_stickbreak_diffattn_block"

def rmsnorm(x, gain):
    xf = x.astype(jnp.float32)
    y = xf * lax.rsqrt(jnp.mean(xf * xf, axis=-1, keepdims=True) + EPS)
    return (y * gain.astype(jnp.float32)).astype(x.dtype)

def alibi_slopes(n_heads):
    return np.array([2.0 ** (-8.0 * (h + 1) / n_heads) for h in range(n_heads)], dtype=np.float32)

def stick_breaking_attention(q, k, v):
    s_len, d = q.shape[1], q.shape[3]
    scale = d ** -0.5
    outs = []
    for i0 in range(0, s_len, Q_BLOCK):
        i1 = i0 + Q_BLOCK
        qb, kb, vb = q[:, i0:i1], k[:, :i1], v[:, :i1]
        z = jnp.einsum('bqhd,bkhd->bhqk', qb, kb).astype(jnp.float32) * scale
        t_idx = np.arange(i0, i1)[:, None]
        s_idx = np.arange(i1)[None, :]
        strict = s_idx < t_idx
        log_keep = jnp.where(strict, jax.nn.log_sigmoid(-z), 0.0)
        after = lax.cumsum(log_keep, axis=3, reverse=True) - log_keep
        w = jnp.where(strict, jnp.exp(jax.nn.log_sigmoid(z) + after), 0.0)
        outs.append(jnp.einsum('bhqk,bkhd->bqhd', w.astype(v.dtype), vb))
    return jnp.concatenate(outs, axis=1)

def differential_attention(q, k, v, lam, head_gain, lambda_init):
    s_len, n_heads, d = q.shape[1], q.shape[2], q.shape[4]
    scale = d ** -0.5
    slopes = alibi_slopes(n_heads)[:, None, None]
    outs = []
    for i0 in range(0, s_len, Q_BLOCK):
        i1 = i0 + Q_BLOCK
        qb, kb, vb = q[:, i0:i1], k[:, :i1], v[:, :i1]
        logits = jnp.einsum('bqhcd,bkhcd->bchqk', qb, kb).astype(jnp.float32) * scale
        t_idx = np.arange(i0, i1)[:, None]
        s_idx = np.arange(i1)[None, :]
        dist = np.abs(t_idx - s_idx).astype(np.float32)
        chunk_mask = (s_idx // CHUNK) <= (t_idx // CHUNK)
        logits = jnp.where(chunk_mask, logits - slopes * dist, -jnp.inf)
        p = jax.nn.softmax(logits, axis=-1)
        w = p[:, 0] - lam * p[:, 1]
        outs.append(jnp.einsum('bhqk,bkhe->bqhe', w.astype(v.dtype), vb))
    o = jnp.concatenate(outs, axis=1)
    return rmsnorm(o, head_gain) * (1.0 - lambda_init)

def setup_inputs(seed: int = 0) -> dict:
    key = jax.random.key(seed)
    ks = jax.random.split(key, 14)
    f32 = jnp.float32
    nrm = lambda k, shape, s: jax.random.normal(k, shape, f32) * s
    return {
        "x": jax.random.normal(ks[0], (BATCH, SEQ, D_MODEL), f32),
        "norm_pre": 1.0 + nrm(ks[1], (DEPTH, D_MODEL), 0.02),
        "norm_post": 1.0 + nrm(ks[2], (DEPTH, D_MODEL), 0.02),
        "w_in": nrm(ks[3], (DEPTH, D_MODEL, IN_COLS), D_MODEL ** -0.5),
        "w_gate": nrm(ks[4], (DEPTH, D_MODEL, N_BRANCH * D_MODEL), D_MODEL ** -0.5),
        "b_gate": nrm(ks[5], (DEPTH, N_BRANCH * D_MODEL), 0.01),
        "w_branch_sb": nrm(ks[6], (DEPTH, SB_WIDTH, D_MODEL), SB_WIDTH ** -0.5),
        "w_branch_df": nrm(ks[7], (DEPTH, DF_WIDTH, D_MODEL), DF_WIDTH ** -0.5),
        "w_out": nrm(ks[8], (DEPTH, D_MODEL, D_MODEL), D_MODEL ** -0.5),
        "lambda_q": nrm(ks[9], (DEPTH, 2, DF_HEAD_DIM), 0.1),
        "lambda_k": nrm(ks[10], (DEPTH, 2, DF_HEAD_DIM), 0.1),
        "df_head_norm": 1.0 + nrm(ks[11], (DEPTH, DF_V_DIM), 0.02),
    }

def reference(x, norm_pre, norm_post, w_in, w_gate, b_gate, w_branch_sb, w_branch_df,
              w_out, lambda_q, lambda_k, df_head_norm):
    b, s, _ = x.shape
    for l in range(DEPTH):
        lambda_init = 0.8 - 0.6 * float(np.exp(-0.3 * l))
        h = rmsnorm(x, norm_pre[l])
        proj = h @ w_in[l]
        sb_q, sb_k, sb_v, sb_z, df_q, df_k, df_v, df_z = jnp.split(proj, IN_SPLITS, axis=-1)

        sb_shape = (b, s, SB_HEADS, SB_HEAD_DIM)
        o_sb = stick_breaking_attention(sb_q.reshape(sb_shape), sb_k.reshape(sb_shape),
                                        sb_v.reshape(sb_shape)).reshape(b, s, SB_WIDTH)
        y_sb = (o_sb * jax.nn.silu(sb_z)) @ w_branch_sb[l]

        lq = lambda_q[l].astype(jnp.float32)
        lk = lambda_k[l].astype(jnp.float32)
        lam = jnp.exp(jnp.sum(lq[0] * lk[0])) - jnp.exp(jnp.sum(lq[1] * lk[1])) + lambda_init
        qk_shape = (b, s, DF_HEADS, 2, DF_HEAD_DIM)
        o_df = differential_attention(df_q.reshape(qk_shape), df_k.reshape(qk_shape),
                                      df_v.reshape(b, s, DF_HEADS, DF_V_DIM), lam,
                                      df_head_norm[l], lambda_init).reshape(b, s, DF_WIDTH)
        y_df = (o_df * jax.nn.silu(df_z)) @ w_branch_df[l]

        gates = jax.nn.sigmoid(h @ w_gate[l] + b_gate[l])
        g_sb, g_df = jnp.split(gates, N_BRANCH, axis=-1)
        out = (g_sb * y_sb + g_df * y_df) @ w_out[l]
        x = x + rmsnorm(out, norm_post[l])
    return x


_drawn_inputs = setup_inputs


def setup_inputs(seed=0):
    import zlib

    import numpy as np

    out = dict(_drawn_inputs(seed))
    spreads = {}
    factors = {'norm_post': 3.939, 'b_gate': 8.0, 'lambda_q': 8.0, 'df_head_norm': 4.803}
    for name, (base, spread) in spreads.items():
        noise = np.random.default_rng([zlib.crc32(name.encode()), seed]).standard_normal(out[name].shape)
        drawn = base * np.exp(spread * noise) if base else spread * noise
        out[name] = __import__('jax').numpy.asarray(drawn.astype(out[name].dtype))
    for name, factor in factors.items():
        out[name] = (out[name] * factor).astype(out[name].dtype)
    return out
```

```python
from contextlib import ExitStack

import concourse.bass as bass
from concourse import mybir

F32 = mybir.dt.float32
F32R = mybir.dt.float32r
ALU = mybir.AluOpType
ACT = mybir.ActivationFunctionType
AX = mybir.AxisListType

P = 128
S = 1024
D = 1024
KC = D // P
NT = S // P
HALF = 512
HD = 64
EPS = 1e-6
LAMBDA_INIT = 0.8 - 0.6 * 1.0
NEG = -float(2 ** 100)
SB_UNITS, DF_UNITS = 4, 4
UNITS = SB_UNITS + DF_UNITS
G_QKV = 6
G_Z0 = UNITS * G_QKV
G_FIN0 = G_Z0 + 2 * UNITS
G_OUT0 = G_FIN0 + 6 * KC
GRANULES = G_OUT0 + 2 * KC
RAW = 4
SPLIT = 2

SB_SLOTS = [(h, i) for h in range(2) for i in range(NT)]
DF_SLOTS = [(0, i) for i in range(NT)]
SB_CHUNKS = [2, 0, 0, 1, 1, 1, 1, 1, 1, 0, 0, 1, 1, 1, 1, 0, 0]
DF_CHUNKS = [2, 1, 1, 1, 1, 2, 2, 2, 0]


def transposes_of(slots):
    out = []
    for _, i in slots:
        blocks = list(range(i, NT))
        out.append([blocks[a:a + 4] for a in range(0, len(blocks), 4)])
    return out


class Kind:

    def __init__(self, name, slots, chunks):
        self.name, self.slots = name, slots
        self.uses = transposes_of(slots)
        self.first_use = []
        n = 2
        for u in self.uses:
            self.first_use.append(n)
            n += len(u)
        self.per_t = n
        self.per_w = len(slots)
        self.per_g = len(slots) // 2
        self.chunks, at = [], 0
        for c in chunks:
            self.chunks.append(list(range(at, at + c)))
            at += c


SB = Kind("sb", SB_SLOTS, SB_CHUNKS)
DF = Kind("df", DF_SLOTS, DF_CHUNKS)


class Unit:

    def __init__(self, kind, i):
        self.kind, self.i = kind, i
        sb = kind is SB
        self.sb = sb
        self.u = i if sb else i + SB_UNITS
        self.base_t = (0 if sb else SB_UNITS * SB.per_t)
        self.base_w = (0 if sb else SB_UNITS * SB.per_w)
        self.base_g = (0 if sb else SB_UNITS * SB.per_g)

    def t(self, n):
        return self.i * self.kind.per_t + (self.base_t + n)

    def w(self, n):
        return self.i * self.kind.per_w + (self.base_w + n)

    def g(self, n):
        return self.i * self.kind.per_g + (self.base_g + n)

    def per(self, count, n):
        return self.u * count + n


def build(nc, x, w_all, norm_pre, norm_post, b_gate, lam_q, lam_k, head_norm, out, o_dram):
    ctx = ExitStack()
    with ctx:
        def sbuf(name, shape, dt=F32, c=None):
            return (c or ctx).enter_context(nc.sbuf_tensor(name, shape, dt))

        def psum(name, shape, c):
            return c.enter_context(nc.psum_tensor(name, shape, F32))

        def sem(name):
            return ctx.enter_context(nc.semaphore(name))

        hT_hi = sbuf("hT_hi", [P, KC, S], F32R)
        hT_lo = sbuf("hT_lo", [P, KC, S], F32R)
        raw = sbuf("raw", [P, RAW, HALF])
        whi = sbuf("whi", [P, SPLIT, HALF], F32R)
        wlo = sbuf("wlo", [P, SPLIT, HALF], F32R)
        zeros = sbuf("zeros", [P, HALF])
        ident = sbuf("ident", [P, P])
        gain_pre = sbuf("gain_pre", [P, KC])
        bias_gate = sbuf("bias_gate", [P, 2 * KC])
        gain_head = sbuf("gain_head", [P, 1])
        small = sbuf("small", [P, 64])
        eps_col = small[:, 0:1]
        neg_lam = small[:, 1:2]
        lam_dot = small[:, 2:4]
        lam_exp = small[:, 4:6]
        sumsq = small[:, 8:16]
        std = small[:, 16:24]
        rstd = small[:, 24:32]
        stats = small[:, 32:52].rearrange("p (b n) -> p b n", b=2)

        attn = ExitStack()
        stack = sbuf("stack", [P, 2, 3, S], F32R, attn)
        stage_hi = sbuf("stage_hi", [P, 2, S], F32R, attn)
        stage_lo = sbuf("stage_lo", [P, 2, S], F32R, attn)
        v_hi = sbuf("v_hi", [P, NT, 192], F32R, attn)
        v_lo = sbuf("v_lo", [P, NT, 192], F32R, attn)
        vT = sbuf("vT", [P, S], F32, attn)
        o_sb = sbuf("o_sb", [P, S], F32, attn)
        alibi = sbuf("alibi", [P, S], F32, attn)
        ident_r = sbuf("ident_r", [P, P], F32R, attn)
        neg_mask = sbuf("neg_mask", [P, 3 * P], F32R, attn)
        pre = ExitStack()
        xt = sbuf("xt", [P, NT, S], F32, pre)
        junk = sbuf("junk", [P, S], F32, pre)
        lam_in = sbuf("lam_in", [P, 2, 2, HD], F32, pre)
        pre.close()
        wT_hi = [sbuf(f"wT_hi{b}", [P, n, 2 * P], F32R, attn) for b, n in enumerate((8, 6))]
        wT_lo = [sbuf(f"wT_lo{b}", [P, n, 2 * P], F32R, attn) for b, n in enumerate((8, 6))]
        keep = [sbuf(f"keep{b}", [P, S + 4], F32, attn) for b in range(2)]
        beta = [sbuf(f"beta{b}", [P, S], F32, attn) for b in range(2)]
        attn.close()

        late = ExitStack()
        gated_hi = sbuf("gated_hi", [P, UNITS, S], F32R, late)
        gated_lo = sbuf("gated_lo", [P, UNITS, S], F32R, late)
        merged = sbuf("merged", [P, KC, S], F32, late)
        zphase = ExitStack()
        o_in = sbuf("o_in", [P, S], F32, zphase)
        silu = sbuf("silu", [P, 2, HALF], F32, zphase)
        sq = sbuf("sq", [P, HALF], F32, zphase)
        sq_hi = sbuf("sq_hi", [P, HALF], F32R, zphase)
        sq_lo = sbuf("sq_lo", [P, HALF], F32R, zphase)
        mean_w = sbuf("mean_w", [P, P], F32R, zphase)
        rms = sbuf("rms", [P, S], F32, zphase)
        zphase.close()
        gate = sbuf("gate", [P, 4, HALF], F32, late)
        late.close()
        tail = ExitStack()
        sbuf("under_merged", [P, 2, UNITS, S], F32, tail)
        tail.close()
        tail = ExitStack()
        x_again = sbuf("x_again", [P, 4, S], F32, tail)
        post = sbuf("post", [P, S], F32, tail)
        junk2 = sbuf("junk2", [P, HALF], F32, tail)
        tail.close()

        pa = ExitStack()
        proj_ps = psum("proj_ps", [P, S], pa)
        score_ps = [psum(f"score_ps{b}", [P, S], pa) for b in range(2)]
        t_ps = psum("t_ps", [P, HALF], pa)
        o_ps = psum("o_ps", [P, HALF], pa)
        pa.close()
        pb = ExitStack()
        bank = psum("bank", [P, 8, HALF], pb)
        pb.close()
        mean_ps = score_ps[0]

        x_loaded = [sem(f"x_loaded{t}") for t in range(NT)]
        const_loaded = sem("const_loaded")
        lam_loaded = sem("lam_loaded")
        raw_loaded = [sem(f"raw_loaded{b}") for b in range(RAW)]
        consts = sem("consts")
        consts_fixed = sem("consts_fixed")
        w_hi_done = sem("w_hi_done")
        w_ready = sem("w_ready")
        halves_done = sem("halves_done")
        sumsq_done = sem("sumsq_done")
        std_done = sem("std_done")
        rstd_done = sem("rstd_done")
        x_normed = sem("x_normed")
        hT_ps_done = sem("hT_ps_done")
        hT_hi_done = sem("hT_hi_done")
        hT_done = sem("hT_done")
        pads_done = sem("pads_done")
        lam_step = sem("lam_step")
        lam_exp_done = sem("lam_exp_done")
        stage_hi_done = sem("stage_hi_done")
        proj_read = sem("proj_read")
        stack_loaded = [[sem(f"stack_loaded{h}{n}") for n in range(2)] for h in range(2)]
        scores_done = sem("scores_done")
        keep_done = sem("keep_done")
        scan_done = sem("scan_done")
        sb_scores_read = sem("sb_scores_read")
        df_scores_read = sem("df_scores_read")
        negmax_done = sem("negmax_done")
        exp_done = sem("exp_done")
        recip_done = sem("recip_done")
        scaled = sem("scaled")
        row_ready = sem("row_ready")
        t_full = sem("t_full")
        t_hi_done = sem("t_hi_done")
        t_free = sem("t_free")
        av_done = sem("av_done")
        o_saved = sem("o_saved")
        o_stored = sem("o_stored")
        z_sig = sem("z_sig")
        z_gated = sem("z_gated")
        z_hi = sem("z_hi")
        z_done = sem("z_done")
        o_loaded = sem("o_loaded")
        z_silu = sem("z_silu")
        sq_done = sem("sq_done")
        sq_hi_done = sem("sq_hi_done")
        sq_split = sem("sq_split")
        mean_done = sem("mean_done")
        rms_done = sem("rms_done")
        normed = sem("normed")
        gates_done = sem("gates_done")
        y_read = sem("y_read")
        merged_done = sem("merged_done")
        m_hi_done = sem("m_hi_done")
        m_done = sem("m_done")
        out_ps = sem("out_ps")
        y_saved = sem("y_saved")
        y_sq = sem("y_sq")
        y_std = sem("y_std")
        fin_step = sem("fin_step")
        y_scaled = sem("y_scaled")
        late_loaded = sem("late_loaded")
        xr_loaded = [sem(f"xr_loaded{b}") for b in range(4)]
        fin_done = sem("fin_done")
        out_stored = [sem(f"out_stored{b}") for b in range(4)]
        waited = sem("waited")

        f32 = lambda ap: ap.bitcast(F32)

        def score_columns(i):
            c0 = 2 * P * (i // 2)
            return [(c0, HALF), (HALF, S)] if c0 < HALF else [(c0, S)]

        block = ctx.enter_context(nc.Block())

        @block.sync
        def _(sp):
            for t in range(NT):
                sp.dma_start(xt[:, t, :], x[t * P:(t + 1) * P, :]).then_inc(x_loaded[t], 16)
                if t == 0:
                    sp.dma_start(gain_pre[:], norm_pre).then_inc(const_loaded, 16)
                    sp.dma_start(bias_gate[:], b_gate).then_inc(const_loaded, 16)
                    sp.dma_start(gain_head[:], head_norm).then_inc(const_loaded, 16)
            for n, src in enumerate((lam_q, lam_k)):
                sp.dma_start(lam_in[:, n], src.partition_broadcast(P)).then_inc(lam_loaded, 16)
            for s in range(RAW):
                sp.dma_start(raw[:, s, :], w_all[s]).then_inc(raw_loaded[s], 16)
            with sp.Fori(1, GRANULES // RAW) as it:
                for s in range(RAW):
                    sp.wait_ge(w_ready, it * RAW + (s + 1 - RAW))
                    sp.dma_start(raw[:, s, :], w_all[it * RAW + s]).then_inc(raw_loaded[s], 16)
            sp.wait_ge(halves_done, 2 * G_OUT0)
            sp.dma_start(post[:], norm_post.partition_broadcast(P)).then_inc(late_loaded, 16)
            for t in range(NT):
                if t >= 4:
                    sp.wait_ge(out_stored[t % 4], 16)
                sp.dma_start(x_again[:, t % 4, :], x[t * P:(t + 1) * P, :]).then_inc(xr_loaded[t % 4], 16)
                if t >= 3:
                    k = t - 3
                    sp.wait_ge(fin_done, k + 1)
                    sp.dma_start(out[k * P:(k + 1) * P, :], x_again[:, k % 4, :]).then_inc(out_stored[k % 4], 16)
            for k in range(NT - 3, NT):
                sp.wait_ge(fin_done, k + 1)
                sp.dma_start(out[k * P:(k + 1) * P, :], x_again[:, k % 4, :]).then_inc(out_stored[k % 4], 16)
            for b in range(4):
                sp.wait_ge(out_stored[b], 16 * NT // 4)

        @block.gpsimd
        def _(pool):
            pool.memset(zeros[:], 0.0).then_inc(consts, 1)
            pool.memset(ident[:], 0.0).then_inc(consts, 1)
            pool.wait_ge(consts, 2)
            pool.affine_select(out=ident[:], in_=ident[:], compare_op=ALU.not_equal, fill=1.0, base=0,
                               pattern=[[-1, P]], channel_multiplier=1).then_inc(consts, 1)
            pool.iota(alibi[:], pattern=[[-1, S]], base=0, channel_multiplier=1,
                      allow_small_or_imprecise_dtypes=True).then_inc(consts, 1)

            def split(g, s, wait_used):
                pool.wait_ge(raw_loaded[s], g_loads(g, s))
                if wait_used:
                    pool.wait_ge(halves_done, g * 2 + 2 * (1 - SPLIT))
                pool.tensor_tensor(whi[:, s % SPLIT, :], raw[:, s, :], zeros[:], ALU.add).then_inc(w_hi_done, 1)
                pool.wait_ge(w_hi_done, g + 1)
                pool.tensor_tensor(wlo[:, s % SPLIT, :], raw[:, s, :], f32(whi[:, s % SPLIT, :]),
                                   ALU.subtract).then_inc(w_ready, 1)

            loads = [16]

            def g_loads(g, s):
                return loads[0]

            for s in range(RAW):
                split(s, s, s >= SPLIT)
            with pool.Fori(1, GRANULES // RAW) as it:
                loads[0] = it * 16 + 16
                for s in range(RAW):
                    split(it * RAW + s, s, True)

        @block.tensor
        def _(pe):
            def three(ps, a_hi, a_lo, b_hi, b_lo, first, last):
                pe.matmul(ps, a_hi, b_hi, start=first, stop=False)
                pe.matmul(ps, a_hi, b_lo, start=False, stop=False)
                return pe.matmul(ps, a_lo, b_hi, start=False, stop=last)

            for half in range(2):
                pe.wait_ge(x_normed, 4 * half + 4)
                for k in range(KC):
                    if half == 0 and k == 0:
                        pe.wait_ge(consts, 3)
                    if half:
                        pe.wait_ge(hT_done, k + 1)
                    for t in range(4):
                        mm = pe.transpose(bank[:, k, t * P:(t + 1) * P],
                                          xt[:, 4 * half + t, k * P:(k + 1) * P], ident[:])
                    mm.then_inc(hT_ps_done, 1)
            pe.wait_ge(hT_done, 2 * KC)
            pe.sem_inc(av_done, 2)

            def w_tile(a, kk):
                return (whi[:, a, kk * P:(kk + 1) * P], wlo[:, a, kk * P:(kk + 1) * P])

            def project(g0, half0, c, skip_wait=False):
                a, n = (c % 4) // 2, c % 2
                if n == 0:
                    pe.wait_ge(w_ready, g0 + (a + 1))
                if a == 0 and not skip_wait:
                    pe.wait_ge(proj_read, half0 + (n - 1))
                ps = proj_ps[:, n * HALF:(n + 1) * HALF]
                for kk in range(4):
                    k = 4 * a + kk
                    hi, lo = w_tile(a, kk)
                    mm = three(ps, hi, lo, hT_hi[:, k, n * HALF:(n + 1) * HALF],
                               hT_lo[:, k, n * HALF:(n + 1) * HALF], k == 0, k == KC - 1)
                mm.then_inc(halves_done, 1)

            def project_chunk(v, c):
                b = c // 4
                project(v * G_QKV + 2 * b, v * 6 + 2 * b, c, skip_wait=isinstance(v, int) and v == 0 and b == 0)

            def transpose_v(un, n):
                pe.wait_ge(t_free, un.t(n + 1))
                if n == 0:
                    pe.wait_ge(proj_read, un.per(6, 6))
                for b in range(4):
                    j = 4 * n + b
                    mm = pe.transpose(t_ps[:, b * P:(b + 1) * P], vT[:, j * P:(j + 1) * P], ident[:])
                mm.then_inc(t_full, 1)

            def scores(un, n):
                h, i = (n // NT, n % NT) if un.sb else (n % 2, n // 2)
                free = sb_scores_read if un.sb else df_scores_read
                pe.wait_ge(free, un.i * 16 + (n + 1))
                need0 = (0, 1) if i < 4 else (1,)
                if (i == 0):
                    for part in need0:
                        pe.wait_ge(stack_loaded[h][part], un.per(64, 64))
                ps = score_ps[n % 2]
                for m, (c0, c1) in enumerate(score_columns(i)):
                    o = ps[:, c0:c1]
                    kk = stack[:, h, 2, c0:c1]
                    q1 = stack[:, h, 0, i * P:(i + 1) * P]
                    q2 = stack[:, h, 1, i * P:(i + 1) * P]
                    pe.matmul(o, q1, kk, start=True, stop=False)
                    if un.sb and m == 0:
                        mask = neg_mask[:, P:3 * P] if i % 2 == 0 else neg_mask[:, 0:2 * P]
                        pe.matmul(ps[:, c0:c0 + 2 * P], ident_r[:], mask, start=False, stop=False)
                    mm = pe.matmul(o, q2, kk, start=False, stop=True)
                mm.then_inc(scores_done, 1)

            def transpose_row(un, n, k):
                h, i = un.kind.slots[n]
                pe.wait_ge(t_free, un.t(un.kind.first_use[n] + k + 1))
                if k == 0:
                    pe.wait_ge(row_ready, un.w(n + 1))
                for b, j in enumerate(un.kind.uses[n][k]):
                    mm = pe.transpose(t_ps[:, b * P:(b + 1) * P], beta[n % 2][:, (j - i) * P:(j - i + 1) * P],
                                      ident[:])
                mm.then_inc(t_full, 1)

            def attend(un, grp):
                h, i0 = un.kind.slots[2 * grp]
                pe.wait_ge(t_free, un.t(un.kind.first_use[2 * grp + 1] + len(un.kind.uses[2 * grp + 1]) + 1))
                pe.wait_ge(o_saved, un.g(grp + 1))
                c0 = 64 * h
                for jr in range(NT - i0):
                    j = i0 + jr
                    mm = three(o_ps[:, 0:2 * P], v_hi[:, j, c0:c0 + P], v_lo[:, j, c0:c0 + P],
                               wT_hi[grp % 2][:, jr, :], wT_lo[grp % 2][:, jr, :], jr == 0, j == NT - 1)
                mm.then_inc(av_done, 1)

            def unit(un, nxt):
                ns = len(un.kind.slots)
                ahead = 1 if un.sb else 2
                transpose_v(un, 0)
                for n in range(2):
                    scores(un, n)
                transpose_v(un, 1)
                if nxt is not None:
                    for c in un.kind.chunks[0]:
                        project_chunk(nxt, c)
                for n in range(ns):
                    transpose_row(un, n, 0)
                    if un.sb and n + 2 < ns:
                        scores(un, n + 2)
                    if not un.sb and n + 1 < ns:
                        for c in range(2):
                            scores(un, 2 * (n + 1) + c)
                    if n >= 2 and n % 2 == 0:
                        attend(un, n // 2 - 1)
                    if nxt is not None:
                        for c in un.kind.chunks[n + 1]:
                            project_chunk(nxt, c)
                    for k in range(1, len(un.kind.uses[n])):
                        transpose_row(un, n, k)
                attend(un, ns // 2 - 1)

            for c in range(12):
                project_chunk(0, c)
            pe.wait_ge(pads_done, 1)
            with pe.Fori(0, SB_UNITS) as i:
                unit(Unit(SB, i), i + 1)
            with pe.Fori(0, DF_UNITS - 1) as i:
                unit(Unit(DF, i), i + (SB_UNITS + 1))
            unit(Unit(DF, DF_UNITS - 1), None)

            def z_unit(v, j, df):
                for c in range(4):
                    if df and c == 2:
                        for n in range(2):
                            pe.wait_ge(sq_split, j * 2 + (n + 1))
                            o = mean_ps[:, n * HALF:(n + 1) * HALF]
                            pe.matmul(o, mean_w[:], sq_hi[:], start=True, stop=False)
                            pe.matmul(o, mean_w[:], sq_lo[:], start=False, stop=True).then_inc(mean_done, 1)
                    project(v * 2 + G_Z0, v * 2 + 6 * UNITS, c)
            with pe.Fori(0, SB_UNITS) as i:
                z_unit(i, i, False)
            with pe.Fori(0, DF_UNITS) as i:
                z_unit(i + SB_UNITS, i, True)

            with pe.Fori(0, KC) as m:
                for b in range(2):
                    for a in range(2):
                        pe.wait_ge(w_ready, m * 6 + (G_FIN0 + 2 * b + a + 1))
                        for n in range(2):
                            if a == 0:
                                pe.wait_ge(gates_done, m * 4 + (2 * b + n + 1))
                            for kk in range(4):
                                k = 4 * a + kk
                                hi, lo = w_tile(a, kk)
                                mm = three(bank[:, 2 * b + n, :], hi, lo, hT_hi[:, k, n * HALF:(n + 1) * HALF],
                                           hT_lo[:, k, n * HALF:(n + 1) * HALF], k == 0, k == KC - 1)
                            mm.then_inc(halves_done, 1)
                for b in range(2):
                    pe.wait_ge(w_ready, m * 6 + (G_FIN0 + 4 + b + 1))
                    if b == 0:
                        pe.wait_ge(z_done, 2 * UNITS + 2)
                    for n in range(2):
                        pe.wait_ge(y_read, m * 4 + (2 * b + n + 1))
                        for kk in range(4):
                            hi, lo = w_tile(b, kk)
                            mm = three(bank[:, 4 + 2 * b + n, :], hi, lo,
                                       gated_hi[:, 4 * b + kk, n * HALF:(n + 1) * HALF],
                                       gated_lo[:, 4 * b + kk, n * HALF:(n + 1) * HALF], kk == 0, kk == 3)
                        mm.then_inc(halves_done, 1)

            for n in range(2):
                for k in range(KC):
                    g = G_OUT0 + n * KC + k
                    pe.wait_ge(w_ready, g + 1)
                    if n == 0:
                        pe.wait_ge(m_done, k + 1)
                    for t in range(NT):
                        if k == 0 and n == 0:
                            pe.wait_ge(*((gates_done, 4 * KC + 4) if t < 4 else (y_read, 4 * KC + 4)))
                        if k == 0 and n == 1:
                            pe.wait_ge(y_saved, t + 1)
                        mm = three(bank[:, t, :], hT_hi[:, k, t * P:(t + 1) * P], hT_lo[:, k, t * P:(t + 1) * P],
                                   whi[:, g % SPLIT, :], wlo[:, g % SPLIT, :], k == 0, k == KC - 1)
                        if k == KC - 1 and t < NT - 1:
                            mm.then_inc(out_ps, 1)
                        elif t == NT - 1:
                            mm.then_inc(halves_done, 2)

        @block.scalar
        def _(act):
            def copy(dst, src, scale=1.0):
                return act.activation(dst, src, ACT.Copy, scale=scale)

            act.sem_inc(sb_scores_read, 2)
            act.sem_inc(o_saved, 1)
            act.sem_inc(o_stored, 16)

            act.wait_ge(consts_fixed, 1)
            for half in range(2):
                for t in range(4 * half, 4 * half + 4):
                    act.wait_ge(x_loaded[t], 16)
                    if t:
                        act.wait_ge(sumsq_done, t)
                    act.activation(junk[:], xt[:, t, :], ACT.Square,
                                   accum_out=sumsq[:, t:t + 1]).then_inc(sumsq_done, 1)
                act.wait_ge(sumsq_done, 4 * half + 4)
                act.activation(std[:, 4 * half:4 * half + 4], sumsq[:, 4 * half:4 * half + 4], ACT.Sqrt,
                               bias=eps_col, scale=1.0 / D).then_inc(std_done, 1)
            act.wait_ge(const_loaded, 48)
            for q in range(2 * KC):
                half, k = q // KC, q % KC
                act.wait_ge(hT_ps_done, q + 1)
                act.activation(hT_hi[:, k, half * HALF:(half + 1) * HALF], bank[:, k, :], ACT.Copy,
                               scale=gain_pre[:, k:k + 1]).then_inc(hT_hi_done, 1)
            act.wait_ge(lam_step, 2)
            act.activation(lam_exp, lam_dot, ACT.Exp).then_inc(lam_exp_done, 1)

            def stage(v, c):
                b, n = c // 4, c % 2
                if b == 2 or (c % 4) < 2:
                    return
                act.wait_ge(halves_done, v * (2 * G_QKV) + (2 * (2 * b + 1) + n + 1))
                if b == 0 and n == 0 and not (isinstance(v, int) and v == 0):
                    for h in range(2):
                        for part in range(2):
                            act.wait_ge(stack_loaded[h][part], v * 64)
                copy(stage_hi[:, b, n * HALF:(n + 1) * HALF], proj_ps[:, n * HALF:(n + 1) * HALF],
                     HD ** -0.5 if b == 0 else 1.0).then_inc(stage_hi_done, 1)

            def load_stack(v, h, part):
                act.wait_ge(stage_hi_done, v * 4 + 4)
                act.wait_ge(proj_read, v * 6 + 4)
                cols = slice(part * HALF, (part + 1) * HALF)
                mine = slice(64 * h, 64 * h + 64)
                top, bottom = slice(0, 64), slice(64, 128)
                done = stack_loaded[h][part]
                act.dma_start(f32(stack[top, h, 0:3:2, cols]), f32(stage_hi[mine, :, cols])).then_inc(done, 16)
                act.dma_start(f32(stack[bottom, h, 0:3:2, cols]), f32(stage_lo[mine, :, cols])).then_inc(done, 16)
                act.dma_start(f32(stack[top, h, 1, cols]), f32(stage_lo[mine, 0, cols])).then_inc(done, 16)
                act.dma_start(f32(stack[bottom, h, 1, cols]), f32(stage_hi[mine, 0, cols])).then_inc(done, 16)

            def t_hi(un, n, k):
                kind = un.kind
                h, i = kind.slots[n]
                grp = n // 2
                i0 = kind.slots[2 * grp][1]
                blocks = kind.uses[n][k]
                act.wait_ge(t_full, un.t(kind.first_use[n] + k + 1))
                if n % 2 == 0 and k == 0:
                    act.wait_ge(av_done, un.g(grp + 1))
                j0 = blocks[0] - i0
                copy(wT_hi[grp % 2][:, j0:j0 + len(blocks), (n % 2) * P:(n % 2 + 1) * P],
                     t_ps[:, 0:len(blocks) * P].rearrange("p (j c) -> p j c", c=P)).then_inc(t_hi_done, 1)

            def v_hi_part(un, n):
                act.wait_ge(t_full, un.t(n + 1))
                if n == 0:
                    act.wait_ge(av_done, un.g(2))
                dst = v_hi[:, 4 * n:4 * n + 4, :]
                if un.sb:
                    src = t_ps[:].rearrange("p (j a c) -> p j a c", j=4, a=2)
                    copy(dst.rearrange("p j (a c) -> p j a c", a=3)[:, :, 0:3:2, :], src).then_inc(t_hi_done, 1)
                else:
                    copy(dst[:, :, 0:P], t_ps[:].rearrange("p (j c) -> p j c", j=4)).then_inc(t_hi_done, 1)

            def save_o(un, grp):
                h, i0 = un.kind.slots[2 * grp]
                act.wait_ge(av_done, un.g(grp + 3))
                if grp == 0:
                    act.wait_ge(o_stored, un.per(16, 16))
                rows = slice(64 * h, 64 * h + 64) if un.sb else slice(0, P)
                cols = slice(i0 * P, (i0 + 2) * P)
                copy(o_sb[rows, cols], o_ps[rows, 0:2 * P]).then_inc(o_saved, 1)

            def sb_sigmoid(un, n, which):
                h, i = un.kind.slots[n]
                width = S - i * P
                if which == 0:
                    act.wait_ge(scores_done, un.per(16, n + 1))
                    act.wait_ge(t_full, un.t(un.kind.first_use[n - 2] + len(un.kind.uses[n - 2]) if n >= 2 else 1))
                    act.activation(keep[n % 2][:, 1:1 + width], score_ps[n % 2][:, i * P:S], ACT.Sigmoid,
                                   scale=-1.0).then_inc(keep_done, 1)
                else:
                    act.activation(beta[n % 2][:, 0:width], score_ps[n % 2][:, i * P:S],
                                   ACT.Sigmoid).then_inc(sb_scores_read, 1)

            def df_exp(un, n, c):
                h, i = un.kind.slots[n]
                width = S - i * P
                row = (beta, keep)[c][n % 2][:, 0:width]
                if c == 0:
                    act.wait_ge(negmax_done, un.i * NT + (n + 1))
                act.activation(row, row, ACT.Exp, bias=stats[:, n % 2, 2 + c:3 + c],
                               accum_out=stats[:, n % 2, 4 + c:5 + c]).then_inc(exp_done, 1)

            def first(un, n, part):
                if un.sb:
                    sb_sigmoid(un, n, part)
                else:
                    df_exp(un, n, part)

            def unit(un, nxt):
                ns = len(un.kind.slots)
                v_hi_part(un, 0)
                first(un, 0, 0)
                v_hi_part(un, 1)
                first(un, 0, 1)
                if nxt is not None:
                    for c in un.kind.chunks[0]:
                        stage(nxt, c)
                done_chunks = len(un.kind.chunks[0])
                loaded = []
                for n in range(ns):
                    if n + 1 < ns:
                        first(un, n + 1, 0)
                    t_hi(un, n, 0)
                    if n + 1 < ns:
                        first(un, n + 1, 1)
                    for k in range(1, len(un.kind.uses[n])):
                        t_hi(un, n, k)
                    if n >= 2 and n % 2 == 0:
                        save_o(un, n // 2 - 1)
                    if nxt is not None:
                        for c in un.kind.chunks[n + 1]:
                            stage(nxt, c)
                        done_chunks += len(un.kind.chunks[n + 1])
                        if done_chunks < 8:
                            continue
                        for h in range(2):
                            for part in range(2):
                                last = (8 * h + 4 * part + 3) if un.sb else (4 * part + 3)
                                if (h, part) not in loaded and n + 1 > last:
                                    act.wait_ge(scores_done, un.per(16, (last + 1) * (1 if un.sb else 2)))
                                    load_stack(nxt, h, part)
                                    loaded.append((h, part))
                if nxt is not None:
                    for h in range(2):
                        for part in range(2):
                            if (h, part) not in loaded:
                                act.wait_ge(scores_done, un.per(16, 16))
                                load_stack(nxt, h, part)
                save_o(un, ns // 2 - 1)
                act.wait_ge(o_saved, un.g(ns // 2 + 1))
                act.dma_start(o_dram[un.u], o_sb[:]).then_inc(o_stored, 16)

            for c in range(12):
                stage(0, c)
            for h in range(2):
                for part in range(2):
                    load_stack(0, h, part)
            with act.Fori(0, SB_UNITS) as i:
                unit(Unit(SB, i), i + 1)
            with act.Fori(0, DF_UNITS - 1) as i:
                unit(Unit(DF, i), i + (SB_UNITS + 1))
            unit(Unit(DF, DF_UNITS - 1), None)

            act.wait_ge(o_stored, 16 * UNITS + 16)

            def load_o(v):
                act.dma_start(o_in[:], o_dram[v]).then_inc(o_loaded, 16)

            load_o(0)

            def z_unit(v, j, df):
                if df:
                    act.wait_ge(o_loaded, v * 16 + 16)
                    for n in range(2):
                        if n:
                            act.wait_ge(sq_split, j * 2 + n)
                        else:
                            act.wait_ge(z_done, v * 2 + 2)
                        act.activation(sq[:], o_in[:, n * HALF:(n + 1) * HALF], ACT.Square).then_inc(sq_done, 1)
                        act.wait_ge(sq_done, j * 2 + (n + 1))
                        if n:
                            act.wait_ge(mean_done, j * 2 + n)
                        copy(sq_hi[:], sq[:]).then_inc(sq_hi_done, 1)
                    for n in range(2):
                        act.wait_ge(mean_done, j * 2 + (n + 1))
                        act.activation(rms[:, n * HALF:(n + 1) * HALF], mean_ps[:, n * HALF:(n + 1) * HALF],
                                       ACT.Sqrt, bias=eps_col).then_inc(rms_done, 1)
                for n in range(2):
                    act.wait_ge(halves_done, v * 4 + (2 * G_Z0 + 2 + n + 1))
                    act.wait_ge(z_done, v * 2 + (n + 1))
                    act.activation(silu[:, n, :], proj_ps[:, n * HALF:(n + 1) * HALF],
                                   ACT.Sigmoid).then_inc(z_sig, 1)
                for n in range(2):
                    act.wait_ge(z_gated, v * 2 + (n + 1))
                    act.sem_inc(waited, 1)
                    copy(gated_hi[:, v, n * HALF:(n + 1) * HALF], silu[:, n, :]).then_inc(z_hi, 1)

            with act.Fori(0, SB_UNITS) as i:
                z_unit(i, i, False)
                load_o(i + 1)
            with act.Fori(0, DF_UNITS - 1) as i:
                z_unit(i + SB_UNITS, i, True)
                load_o(i + (SB_UNITS + 1))
            z_unit(UNITS - 1, DF_UNITS - 1, True)

            act.wait_ge(z_done, 2 * UNITS + 2)
            act.sem_inc(gates_done, 4)
            with act.Fori(0, KC) as m:
                for b in range(2):
                    for n in range(2):
                        q = 2 * b + n
                        act.wait_ge(halves_done, m * 12 + (2 * (G_FIN0 + 2 * b + 1) + n + 1))
                        act.wait_ge(merged_done, m * 2 + 2)
                        act.sem_inc(waited, 1)
                        act.activation(gate[:, q, :], bank[:, q, :], ACT.Sigmoid,
                                       bias=bias_gate[:, bass.ds(m + b * KC, 1)]).then_inc(gates_done, 1)

            for k in range(KC):
                act.wait_ge(merged_done, 2 * KC + 2)
                copy(hT_hi[:, k, :], merged[:, k, :]).then_inc(m_hi_done, 1)
            for q in range(2 * NT):
                n, t = q // NT, q % NT
                act.wait_ge(y_saved, q + 1)
                if q:
                    act.wait_ge(y_sq, q)
                acc = (sumsq, std)[n][:, t:t + 1]
                act.activation(junk2[:], merged[:, t, n * HALF:(n + 1) * HALF], ACT.Square,
                               accum_out=acc).then_inc(y_sq, 1)
            act.wait_ge(fin_step, 1)
            act.activation(sumsq, sumsq, ACT.Sqrt, bias=eps_col, scale=1.0 / D).then_inc(y_std, 1)

        @block.vector
        def _(dve):
            dve.memset(eps_col, EPS).then_inc(consts_fixed, 1)
            dve.wait_ge(consts, 4)
            dve.tensor_copy(ident_r[:], ident[:])
            dve.memset(f32(neg_mask[:]), 0.0).then_inc(consts_fixed, 1)
            dve.scalar_tensor_tensor(alibi[:], alibi[:], -1.0, alibi[:], ALU.mult, ALU.min).then_inc(consts_fixed, 1)
            dve.tensor_tensor_scan(vT[:, 0:P], ident[:], zeros[:, 0:P], 0.0, ALU.add, ALU.add)\
               .then_inc(consts_fixed, 1)
            dve.wait_ge(consts_fixed, 4)
            dve.tensor_scalar(alibi[:], alibi[:], 0.25, None, ALU.mult).then_inc(consts_fixed, 1)
            dve.tensor_tensor(vT[:, P:2 * P], vT[:, 0:P], ident[:], ALU.subtract).then_inc(consts_fixed, 1)
            dve.wait_ge(consts_fixed, 6)
            dve.memset(alibi[64:128, 0:64], -3e38).then_inc(consts_fixed, 1)
            dve.tensor_scalar(neg_mask[:, P:2 * P], vT[:, P:2 * P], -NEG, NEG, ALU.mult, ALU.add)\
               .then_inc(consts_fixed, 1)
            dve.wait_ge(consts_fixed, 8)
            dve.sem_inc(t_free, 1)

            for half in range(2):
                cols = slice(4 * half, 4 * half + 4)
                dve.wait_ge(std_done, half + 1)
                dve.reciprocal(rstd[:, cols], std[:, cols]).then_inc(rstd_done, 1)
                dve.wait_ge(rstd_done, half + 1)
                for t in range(4 * half, 4 * half + 4):
                    dve.tensor_scalar(xt[:, t, :], xt[:, t, :], rstd[:, t:t + 1], None, ALU.mult)\
                       .then_inc(x_normed, 1)
            dve.wait_ge(lam_loaded, 32)
            dve.tensor_tensor(lam_in[:, 0], lam_in[:, 0], lam_in[:, 1], ALU.mult).then_inc(lam_step, 1)
            dve.wait_ge(lam_step, 1)
            dve.tensor_reduce(lam_dot, lam_in[:, 0], AX.X, ALU.add).then_inc(lam_step, 1)
            dve.wait_ge(const_loaded, 48)
            for q in range(2 * KC):
                half, k = q // KC, q % KC
                cols = slice(half * HALF, (half + 1) * HALF)
                dve.wait_ge(hT_hi_done, q + 1)
                dve.scalar_tensor_tensor(hT_lo[:, k, cols], bank[:, k, :], gain_pre[:, k:k + 1],
                                         f32(hT_hi[:, k, cols]), ALU.mult, ALU.subtract).then_inc(hT_done, 1)
            dve.wait_ge(lam_exp_done, 1)
            dve.tensor_tensor(neg_lam, lam_exp[:, 1:2], lam_exp[:, 0:1], ALU.subtract).then_inc(lam_step, 1)
            dve.wait_ge(lam_step, 3)
            dve.tensor_scalar(neg_lam, neg_lam, -LAMBDA_INIT, None, ALU.add).then_inc(lam_step, 1)
            dve.tensor_scalar(gain_head[:], gain_head[:], 1.0 - LAMBDA_INIT, None, ALU.mult).then_inc(lam_step, 1)
            for b in range(2):
                dve.memset(f32(wT_hi[b][:, 0, P:2 * P]), 0.0)
                dve.memset(f32(wT_lo[b][:, 0, P:2 * P]), 0.0)
                dve.memset(keep[b][:, 0:1], 1.0)
            dve.memset(f32(v_hi[:, :, 64:128]), 0.0)
            dve.memset(f32(v_lo[:, :, 64:128]), 0.0).then_inc(pads_done, 1)

            def stage(v, c):
                b, n = c // 4, c % 2
                if (c % 4) < 2:
                    return
                cols = slice(n * HALF, (n + 1) * HALF)
                ps = proj_ps[:, cols]
                if b == 2:
                    dve.wait_ge(halves_done, v * (2 * G_QKV) + (2 * (2 * b + 1) + n + 1))
                    dve.tensor_copy(vT[:, cols], ps).then_inc(proj_read, 1)
                    return
                dve.wait_ge(stage_hi_done, v * 4 + (2 * b + n + 1))
                if b == 0:
                    dve.scalar_tensor_tensor(stage_lo[:, b, cols], ps, HD ** -0.5, f32(stage_hi[:, b, cols]),
                                             ALU.mult, ALU.subtract).then_inc(proj_read, 1)
                else:
                    dve.tensor_tensor(stage_lo[:, b, cols], ps, f32(stage_hi[:, b, cols]),
                                      ALU.subtract).then_inc(proj_read, 1)

            def t_lo(un, n, k):
                kind = un.kind
                grp = n // 2
                i0 = kind.slots[2 * grp][1]
                blocks = kind.uses[n][k]
                dve.wait_ge(t_hi_done, un.t(kind.first_use[n] + k + 1))
                j0 = blocks[0] - i0
                cols = slice((n % 2) * P, (n % 2 + 1) * P)
                dve.tensor_tensor(wT_lo[grp % 2][:, j0:j0 + len(blocks), cols],
                                  t_ps[:, 0:len(blocks) * P].rearrange("p (j c) -> p j c", c=P),
                                  f32(wT_hi[grp % 2][:, j0:j0 + len(blocks), cols]),
                                  ALU.subtract).then_inc(t_free, 1)

            def v_lo_part(un, n):
                dve.wait_ge(t_hi_done, un.t(n + 1))
                rows = slice(4 * n, 4 * n + 4)
                if un.sb:
                    view = lambda t: t[:, rows, :].rearrange("p j (a c) -> p j a c", a=3)[:, :, 0:3:2, :]
                    src = t_ps[:].rearrange("p (j a c) -> p j a c", j=4, a=2)
                else:
                    view = lambda t: t[:, rows, 0:P]
                    src = t_ps[:].rearrange("p (j c) -> p j c", j=4)
                dve.tensor_tensor(view(v_lo), src, f32(view(v_hi)), ALU.subtract).then_inc(t_free, 1)

            def sb_scan(un, n):
                i = un.kind.slots[n][1]
                width = S - i * P
                k = keep[n % 2][:, 1:1 + width]
                dve.wait_ge(keep_done, un.per(16, n + 1))
                dve.tensor_tensor_scan(k, k, zeros[:, 0:1].to_broadcast([P, width]), 1.0,
                                       ALU.mult, ALU.add).then_inc(scan_done, 1)

            def sb_weights(un, n):
                i = un.kind.slots[n][1]
                width = S - i * P
                dve.wait_ge(sb_scores_read, un.per(16, n + 3))
                dve.wait_ge(scan_done, un.per(16, n + 1))
                dve.tensor_tensor(beta[n % 2][:, 0:width], beta[n % 2][:, 0:width], keep[n % 2][:, 0:width],
                                  ALU.mult).then_inc(row_ready, 1)

            def df_logits(un, n):
                i = un.kind.slots[n][1]
                width = S - i * P
                st = stats[:, n % 2]
                if n >= 2:
                    dve.wait_ge(t_full, un.t(un.kind.first_use[n - 2] + len(un.kind.uses[n - 2])))
                else:
                    dve.wait_ge(t_full, un.t(1))
                for c in range(2):
                    dve.wait_ge(scores_done, un.per(16, 2 * n + c + 1))
                    dve.sem_inc(waited, 1)
                    dve.tensor_tensor_reduce(out=(beta, keep)[c][n % 2][:, 0:width], in0=score_ps[c][:, i * P:S],
                                             in1=alibi[:, 0:width], scale=1.0, scalar=-3.4e38, op0=ALU.add,
                                             op1=ALU.max, accum_out=st[:, c:c + 1]).then_inc(df_scores_read, 1)
                dve.wait_ge(df_scores_read, un.i * 16 + (2 * n + 4))
                dve.tensor_scalar(st[:, 2:4], st[:, 0:2], -1.0, None, ALU.mult).then_inc(negmax_done, 1)

            def df_weights(un, n):
                i = un.kind.slots[n][1]
                width = S - i * P
                st = stats[:, n % 2]
                p1, p2 = beta[n % 2][:, 0:width], keep[n % 2][:, 0:width]
                dve.wait_ge(exp_done, un.i * 16 + (2 * n + 2))
                dve.reciprocal(st[:, 6:8], st[:, 4:6]).then_inc(recip_done, 1)
                dve.wait_ge(recip_done, un.i * NT + (n + 1))
                dve.tensor_scalar(st[:, 8:9], st[:, 7:8], neg_lam, None, ALU.mult).then_inc(scaled, 1)
                dve.tensor_scalar(p1, p1, st[:, 6:7], None, ALU.mult).then_inc(scaled, 1)
                dve.wait_ge(scaled, un.i * 16 + (2 * n + 2))
                dve.scalar_tensor_tensor(p1, p2, st[:, 8:9], p1, ALU.mult, ALU.add).then_inc(row_ready, 1)

            def unit(un, nxt):
                ns = len(un.kind.slots)
                v_lo_part(un, 0)
                if un.sb:
                    sb_scan(un, 0)
                else:
                    df_logits(un, 0)
                v_lo_part(un, 1)
                if un.sb:
                    sb_weights(un, 0)
                else:
                    df_weights(un, 0)
                if nxt is not None:
                    for c in un.kind.chunks[0]:
                        stage(nxt, c)
                for n in range(ns):
                    if n + 1 < ns:
                        if un.sb:
                            sb_scan(un, n + 1)
                        else:
                            df_logits(un, n + 1)
                    t_lo(un, n, 0)
                    if n + 1 < ns and un.sb:
                        sb_weights(un, n + 1)
                    for k in range(1, len(un.kind.uses[n])):
                        t_lo(un, n, k)
                    if n + 1 < ns and not un.sb:
                        df_weights(un, n + 1)
                    if nxt is not None:
                        for c in un.kind.chunks[n + 1]:
                            stage(nxt, c)

            for c in range(12):
                stage(0, c)
            with dve.Fori(0, SB_UNITS) as i:
                unit(Unit(SB, i), i + 1)
            dve.sem_inc(df_scores_read, 2)
            with dve.Fori(0, DF_UNITS - 1) as i:
                unit(Unit(DF, i), i + (SB_UNITS + 1))
                dve.tensor_scalar(alibi[:], alibi[:], 0.25, None, ALU.mult).then_inc(consts_fixed, 1)
                dve.wait_ge(consts_fixed, i + 9)
            unit(Unit(DF, DF_UNITS - 1), None)

            dve.wait_ge(o_stored, 16 * UNITS + 16)
            dve.memset(f32(mean_w[:]), 1.0 / P)
            dve.sem_inc(z_done, 2)

            def z_unit(v, j, df):
                if df:
                    for n in range(2):
                        dve.wait_ge(sq_hi_done, j * 2 + (n + 1))
                        dve.tensor_tensor(sq_lo[:], sq[:], f32(sq_hi[:]), ALU.subtract).then_inc(sq_split, 1)
                    for n in range(2):
                        cols = slice(n * HALF, (n + 1) * HALF)
                        dve.wait_ge(rms_done, j * 2 + (n + 1))
                        dve.reciprocal(rms[:, cols], rms[:, cols]).then_inc(normed, 1)
                        dve.wait_ge(normed, j * 4 + (2 * n + 1))
                        dve.scalar_tensor_tensor(o_in[:, cols], o_in[:, cols], gain_head[:, 0:1], rms[:, cols],
                                                 ALU.mult, ALU.mult).then_inc(normed, 1)
                for n in range(2):
                    cols = slice(n * HALF, (n + 1) * HALF)
                    dve.wait_ge(z_sig, v * 2 + (n + 1))
                    dve.tensor_tensor(silu[:, n, :], proj_ps[:, cols], silu[:, n, :], ALU.mult).then_inc(proj_read, 1)
                    dve.wait_ge(proj_read, v * 2 + (6 * UNITS + n + 1))
                    if n == 0:
                        dve.wait_ge(o_loaded, v * 16 + 16)
                    if df:
                        dve.wait_ge(normed, j * 4 + (2 * n + 2))
                    dve.tensor_tensor(silu[:, n, :], silu[:, n, :], o_in[:, cols], ALU.mult).then_inc(z_gated, 1)
                for n in range(2):
                    cols = slice(n * HALF, (n + 1) * HALF)
                    dve.wait_ge(z_hi, v * 2 + (n + 1))
                    dve.tensor_tensor(gated_lo[:, v, cols], silu[:, n, :], f32(gated_hi[:, v, cols]),
                                      ALU.subtract).then_inc(z_done, 1)

            with dve.Fori(0, SB_UNITS) as i:
                z_unit(i, i, False)
            with dve.Fori(0, DF_UNITS) as i:
                z_unit(i + SB_UNITS, i, True)

            dve.sem_inc(y_read, 4)
            dve.sem_inc(merged_done, 2)
            with dve.Fori(0, KC) as m:
                for b in range(2):
                    for n in range(2):
                        q = 2 * b + n
                        cols = slice(n * HALF, (n + 1) * HALF)
                        dve.wait_ge(halves_done, m * 12 + (2 * (G_FIN0 + 4 + b) + n + 1))
                        if q == 0:
                            dve.wait_ge(gates_done, m * 4 + 8)
                        dst = merged[:, m, cols] if b == 0 else gate[:, q, :]
                        dve.tensor_tensor(dst, bank[:, 4 + q, :], gate[:, q, :], ALU.mult).then_inc(y_read, 1)
                for n in range(2):
                    cols = slice(n * HALF, (n + 1) * HALF)
                    dve.wait_ge(y_read, m * 4 + (n + 7))
                    dve.tensor_tensor(merged[:, m, cols], merged[:, m, cols], gate[:, 2 + n, :],
                                      ALU.add).then_inc(merged_done, 1)
            for k in range(KC):
                dve.wait_ge(m_hi_done, k + 1)
                dve.tensor_tensor(hT_lo[:, k, :], merged[:, k, :], f32(hT_hi[:, k, :]), ALU.subtract)\
                   .then_inc(m_done, 1)
            for q in range(2 * NT):
                n, t = q // NT, q % NT
                if t < NT - 1:
                    dve.wait_ge(out_ps, (NT - 1) * n + t + 1)
                else:
                    dve.wait_ge(halves_done, 2 * (G_OUT0 + KC * (n + 1)))
                dve.wait_ge(m_done, KC)
                dve.tensor_copy(merged[:, t, n * HALF:(n + 1) * HALF], bank[:, t, :]).then_inc(y_saved, 1)
            dve.wait_ge(y_sq, 2 * NT)
            dve.tensor_tensor(sumsq, sumsq, std, ALU.add).then_inc(fin_step, 1)
            dve.wait_ge(y_std, 1)
            dve.reciprocal(rstd, sumsq).then_inc(fin_step, 1)
            dve.wait_ge(fin_step, 2)
            dve.wait_ge(late_loaded, 16)
            for t in range(NT):
                dve.scalar_tensor_tensor(merged[:, t, :], merged[:, t, :], rstd[:, t:t + 1], post[:],
                                         ALU.mult, ALU.mult).then_inc(y_scaled, 1)
                dve.wait_ge(xr_loaded[t % 4], 16 * (t // 4 + 1))
                dve.wait_ge(y_scaled, t + 1)
                dve.tensor_tensor(x_again[:, t % 4, :], x_again[:, t % 4, :], merged[:, t, :],
                                  ALU.add).then_inc(fin_done, 1)


def granules(w_in, w_gate, w_sb, w_df, w_out):
    import numpy as np

    def columns(w, c):
        part = w[:, c:c + P].reshape(-1, 4, P, P)
        return part.transpose(0, 2, 1, 3).reshape(-1, P, HALF)

    def column(u, part):
        return (u // 4) * 2048 + part * 512 + (u % 4) * P

    g = [columns(w_in, column(u, part)) for u in range(UNITS) for part in range(3)]
    g += [columns(w_in, column(u, 3)) for u in range(UNITS)]
    for m in range(KC):
        g += [columns(w_gate, m * P), columns(w_gate, D + m * P), columns(w_sb, m * P), columns(w_df, m * P)]
    g += [w_out[k * P:(k + 1) * P, n * HALF:(n + 1) * HALF][None] for n in range(2) for k in range(KC)]
    return np.ascontiguousarray(np.concatenate(g, axis=0))


def kernel(x, norm_pre, norm_post, w_in, w_gate, b_gate, w_branch_sb, w_branch_df, w_out, lambda_q, lambda_k,
           df_head_norm):
    import numpy as np
    import concourse.bacc as bacc
    from concourse.bass_utils import run_bass_kernel_spmd

    a = {n: np.asarray(v) for n, v in dict(
        x=x, norm_pre=norm_pre, norm_post=norm_post, w_in=w_in, w_gate=w_gate, b_gate=b_gate, w_sb=w_branch_sb,
        w_df=w_branch_df, w_out=w_out, lambda_q=lambda_q, lambda_k=lambda_k, head_norm=df_head_norm).items()}
    cont = np.ascontiguousarray
    ins = {
        "x_rev": cont(a["x"][0, ::-1]),
        "w_all": granules(a["w_in"][0], a["w_gate"][0], a["w_sb"][0], a["w_df"][0], a["w_out"][0]),
        "norm_pre_t": cont(a["norm_pre"][0].reshape(KC, P).T),
        "norm_post_r": cont(a["norm_post"][0]),
        "b_gate_t": cont(a["b_gate"][0].reshape(2 * KC, P).T),
        "lambda_q_r": cont(a["lambda_q"][0]),
        "lambda_k_r": cont(a["lambda_k"][0]),
        "head_norm_t": cont(a["head_norm"][0].reshape(P, 1)),
    }
    nc = bacc.Bacc("TRN2", target_bir_lowering=False, num_devices=1)
    args = [nc.dram_tensor(n, v.shape, mybir.dt.from_np(v.dtype), kind="ExternalInput").ap() for n, v in ins.items()]
    out = nc.dram_tensor("out_rev", (S, D), F32, kind="ExternalOutput").ap()
    o_dram = nc.dram_tensor("o_scratch", (UNITS, P, S), F32, kind="Internal").ap()
    xx, w_all, npre, npost, bg, lq, lk, hn = args
    build(nc, xx, w_all, npre, npost, bg, lq, lk, hn, out, o_dram)
    r = run_bass_kernel_spmd(nc, [ins], core_ids=[0])
    return r.results[0]["out_rev"][::-1].reshape(1, S, D)
```

```python
from contextlib import ExitStack

import concourse.bass as bass
from concourse import mybir

F32 = mybir.dt.float32
F32R = mybir.dt.float32r
ALU = mybir.AluOpType
ACT = mybir.ActivationFunctionType
AX = mybir.AxisListType

P = 128
S = 1024
D = 1024
KC = D // P
NT = S // P
HALF = 512
HD = 64
EPS = 1e-6
LAMBDA_INIT = 0.8 - 0.6 * 1.0
NEG = -float(2 ** 100)
SB_UNITS, DF_UNITS = 4, 4
UNITS = SB_UNITS + DF_UNITS
G_QKV = 6
G_Z0 = UNITS * G_QKV
G_FIN0 = G_Z0 + 2 * UNITS
G_OUT0 = G_FIN0 + 6 * KC
GRANULES = G_OUT0 + 2 * KC
RAW = 6
SPLIT = 2

SB_SLOTS = [(h, i) for h in range(2) for i in range(NT)]
DF_SLOTS = [(0, i) for i in range(NT)]
SB_CHUNKS = [4, 1, 1, 2, 1, 2, 1, 2, 1, 1, 1, 1, 1, 1, 1, 2, 1]
DF_CHUNKS = [4, 1, 2, 2, 3, 3, 3, 3, 3]
LAST_CHUNKS = [4, 2, 2, 3, 3, 3, 3, 3, 3]


def transposes_of(slots):
    out = []
    for _, i in slots:
        blocks = list(range(i, NT))
        out.append([blocks[a:a + 4] for a in range(0, len(blocks), 4)])
    return out


def chunk_parts(c):
    return c // 8, (c % 8) // 4, (c % 4) // 2, c % 2


def completes(c):
    return c % 8 in (5, 7)


def numbered(counts):
    out, at = [], 0
    for c in counts:
        out.append(list(range(at, at + c)))
        at += c
    return out


class Kind:

    def __init__(self, name, slots, chunks):
        self.name, self.slots = name, slots
        self.uses = transposes_of(slots)
        self.first_use = []
        n = 2
        for u in self.uses:
            self.first_use.append(n)
            n += len(u)
        self.per_t = n
        self.per_w = len(slots)
        self.per_g = len(slots) // 2
        self.chunks = numbered(chunks)


SB = Kind("sb", SB_SLOTS, SB_CHUNKS)
DF = Kind("df", DF_SLOTS, DF_CHUNKS)


class Unit:

    def __init__(self, kind, i):
        self.kind, self.i = kind, i
        sb = kind is SB
        self.sb = sb
        self.u = i if sb else i + SB_UNITS
        self.base_t = (0 if sb else SB_UNITS * SB.per_t)
        self.base_w = (0 if sb else SB_UNITS * SB.per_w)
        self.base_g = (0 if sb else SB_UNITS * SB.per_g)

    def t(self, n):
        return self.i * self.kind.per_t + (self.base_t + n)

    def w(self, n):
        return self.i * self.kind.per_w + (self.base_w + n)

    def g(self, n):
        return self.i * self.kind.per_g + (self.base_g + n)

    def per(self, count, n):
        return self.u * count + n


def build(nc, x, w_all, norm_pre, norm_post, b_gate, lam_q, lam_k, head_norm, out, o_dram):
    ctx = ExitStack()
    with ctx:
        def sbuf(name, shape, dt=F32, c=None):
            return (c or ctx).enter_context(nc.sbuf_tensor(name, shape, dt))

        def psum(name, shape, c):
            return c.enter_context(nc.psum_tensor(name, shape, F32))

        def sem(name):
            return ctx.enter_context(nc.semaphore(name))

        hT_hi = sbuf("hT_hi", [P, KC, S], F32R)
        hT_lo = sbuf("hT_lo", [P, KC, S], F32R)
        raw = sbuf("raw", [P, RAW, HALF])
        whi = sbuf("whi", [P, SPLIT, HALF], F32R)
        wlo = sbuf("wlo", [P, SPLIT, HALF], F32R)
        zeros = sbuf("zeros", [P, HALF])
        ident = sbuf("ident", [P, P])
        gain_pre = sbuf("gain_pre", [P, KC])
        bias_gate = sbuf("bias_gate", [P, 2 * KC])
        gain_head = sbuf("gain_head", [P, 1])
        small = sbuf("small", [P, 64])
        eps_col = small[:, 0:1]
        neg_lam = small[:, 1:2]
        lam_dot = small[:, 2:4]
        lam_exp = small[:, 4:6]
        sumsq = small[:, 8:16]
        std = small[:, 16:24]
        rstd = small[:, 24:32]
        stats = small[:, 32:52].rearrange("p (b n) -> p b n", b=2)

        attn = ExitStack()
        stack = sbuf("stack", [P, 2, 3, S], F32R, attn)
        v_hi = sbuf("v_hi", [P, NT, 192], F32R, attn)
        v_lo = sbuf("v_lo", [P, NT, 192], F32R, attn)
        pre = ExitStack()
        xt = sbuf("xt", [P, NT, S], F32, pre)
        junk = sbuf("junk", [P, S], F32, pre)
        lam_in = sbuf("lam_in", [P, 2, 2, HD], F32, pre)
        pre.close()
        wT_hi = [sbuf(f"wT_hi{b}", [P, n, 2 * P], F32R, attn) for b, n in enumerate((8, 6))]
        wT_lo = [sbuf(f"wT_lo{b}", [P, n, 2 * P], F32R, attn) for b, n in enumerate((8, 6))]
        stage_hi = sbuf("stage_hi", [P, 2, S], F32R, attn)
        stage_lo = sbuf("stage_lo", [P, 2, S], F32R, attn)
        keep = [sbuf(f"keep{b}", [P, S + 4], F32, attn) for b in range(2)]
        beta = [sbuf(f"beta{b}", [P, S], F32, attn) for b in range(2)]
        vT = sbuf("vT", [P, S], F32, attn)
        o_sb = sbuf("o_sb", [P, S], F32, attn)
        alibi = sbuf("alibi", [P, S], F32, attn)
        ident_r = sbuf("ident_r", [P, P], F32R, attn)
        neg_mask = sbuf("neg_mask", [P, 3 * P], F32R, attn)
        attn.close()

        late = ExitStack()
        gated_hi = sbuf("gated_hi", [P, UNITS, S], F32R, late)
        gated_lo = sbuf("gated_lo", [P, UNITS, S], F32R, late)
        zphase = ExitStack()
        early_z = sbuf("early_z", [P, SB_UNITS, S], F32, zphase)
        o_in = [sbuf(f"o_in{b}", [P, S], F32, zphase) for b in range(2)]
        silu = sbuf("silu", [P, 2, HALF], F32, zphase)
        sq = sbuf("sq", [P, HALF], F32, zphase)
        sq_hi = sbuf("sq_hi", [P, HALF], F32R, zphase)
        sq_lo = sbuf("sq_lo", [P, HALF], F32R, zphase)
        mean_w = sbuf("mean_w", [P, P], F32R, zphase)
        rms = sbuf("rms", [P, S], F32, zphase)
        gate = sbuf("gate", [P, 4, HALF], F32, zphase)
        zphase.close()
        merged = sbuf("merged", [P, KC, S], F32, late)
        late.close()
        tail = ExitStack()
        x_again = sbuf("x_again", [P, NT, S], F32, tail)
        post = sbuf("post", [P, S], F32, tail)
        junk2 = sbuf("junk2", [P, HALF], F32, tail)
        tail.close()

        pa = ExitStack()
        proj_ps = psum("proj_ps", [P, S], pa)
        score_ps = [psum(f"score_ps{b}", [P, S], pa) for b in range(2)]
        t_ps = psum("t_ps", [P, HALF], pa)
        o_ps = psum("o_ps", [P, HALF], pa)
        pa.close()
        pb = ExitStack()
        bank = psum("bank", [P, 8, HALF], pb)
        pb.close()
        mean_ps = score_ps[0]

        x_loaded = [sem(f"x_loaded{t}") for t in range(NT)]
        const_loaded = sem("const_loaded")
        lam_loaded = sem("lam_loaded")
        raw_loaded = [sem(f"raw_loaded{b}") for b in range(RAW)]
        consts = sem("consts")
        consts_fixed = sem("consts_fixed")
        w_hi_done = sem("w_hi_done")
        w_ready = sem("w_ready")
        halves_done = sem("halves_done")
        sumsq_done = sem("sumsq_done")
        std_done = sem("std_done")
        rstd_done = sem("rstd_done")
        x_normed = sem("x_normed")
        hT_ps_done = sem("hT_ps_done")
        hT_hi_done = sem("hT_hi_done")
        hT_done = sem("hT_done")
        pads_done = sem("pads_done")
        lam_step = sem("lam_step")
        lam_exp_done = sem("lam_exp_done")
        stage_hi_done = sem("stage_hi_done")
        proj_read = sem("proj_read")
        stack_loaded = [sem(f"stack_loaded{h}") for h in range(2)]
        stack_half = [sem(f"stack_half{n}") for n in range(2)]
        scores_done = sem("scores_done")
        keep_done = sem("keep_done")
        scan_done = sem("scan_done")
        sb_scores_read = sem("sb_scores_read")
        df_scores_read = sem("df_scores_read")
        negmax_done = sem("negmax_done")
        exp_done = sem("exp_done")
        recip_done = sem("recip_done")
        scaled = sem("scaled")
        row_ready = sem("row_ready")
        t_full = sem("t_full")
        t_hi_done = sem("t_hi_done")
        t_free = sem("t_free")
        av_done = sem("av_done")
        o_saved = sem("o_saved")
        o_stored = sem("o_stored")
        z_sig = sem("z_sig")
        z_gated = sem("z_gated")
        z_hi = sem("z_hi")
        z_done = sem("z_done")
        o_loaded = [sem(f"o_loaded{b}") for b in range(2)]
        early_z_done = sem("early_z_done")
        rms_ln = sem("rms_ln")
        z_silu = sem("z_silu")
        sq_done = sem("sq_done")
        sq_hi_done = sem("sq_hi_done")
        sq_split = sem("sq_split")
        mean_done = sem("mean_done")
        rms_done = sem("rms_done")
        normed = sem("normed")
        gates_done = sem("gates_done")
        y_read = sem("y_read")
        merged_done = sem("merged_done")
        m_hi_done = sem("m_hi_done")
        m_done = sem("m_done")
        out_ps = sem("out_ps")
        sq_half = [sem(f"sq_half{n}") for n in range(2)]
        y_post = sem("y_post")
        y_saved = sem("y_saved")
        y_std = sem("y_std")
        fin_step = sem("fin_step")
        y_scaled = sem("y_scaled")
        late_loaded = sem("late_loaded")
        xr_loaded = [sem(f"xr_loaded{t}") for t in range(NT)]
        fin_done = sem("fin_done")
        out_stored = sem("out_stored")
        waited = sem("waited")

        f32 = lambda ap: ap.bitcast(F32)

        def score_columns(i):
            c0 = 2 * P * (i // 2)
            return [(c0, HALF), (HALF, S)] if c0 < HALF else [(c0, S)]

        block = ctx.enter_context(nc.Block())

        @block.sync
        def _(sp):
            for t in range(NT):
                sp.dma_start(xt[:, t, :], x[t * P:(t + 1) * P, :]).then_inc(x_loaded[t], 16)
                if t == 0:
                    sp.dma_start(gain_pre[:], norm_pre).then_inc(const_loaded, 16)
                    sp.dma_start(bias_gate[:], b_gate).then_inc(const_loaded, 16)
                    sp.dma_start(gain_head[:], head_norm).then_inc(const_loaded, 16)
            for n, src in enumerate((lam_q, lam_k)):
                sp.dma_start(lam_in[:, n], src.partition_broadcast(P)).then_inc(lam_loaded, 16)
            def load_granule(n, slot):
                sp.wait_ge(w_ready, n + (1 - RAW))
                sp.dma_start(raw[:, slot, :], w_all[n]).then_inc(raw_loaded[slot], 16)

            def load_stack(v, h, cols, done):
                mine = slice(64 * h, 64 * h + 64)
                top, bottom = slice(0, 64), slice(64, 128)
                for n, (dst, src) in enumerate((
                        (stack[top, h, 0:3:2, cols], stage_hi[mine, :, cols]),
                        (stack[bottom, h, 0:3:2, cols], stage_lo[mine, :, cols]),
                        (stack[top, h, 1, cols], stage_lo[mine, 0, cols]),
                        (stack[bottom, h, 1, cols], stage_hi[mine, 0, cols]))):
                    sem_, inc = done[n % len(done)]
                    sp.dma_start(f32(dst), f32(src)).then_inc(sem_, inc)

            def staged(v):
                sp.wait_ge(stage_hi_done, v * 4 + 4)
                sp.wait_ge(proj_read, v * 6 + 4)

            everything = slice(0, S)
            for s in range(RAW):
                sp.dma_start(raw[:, s, :], w_all[s]).then_inc(raw_loaded[s], 16)
            for s in range(RAW):
                load_granule(RAW + s, s)
            staged(0)
            for h in range(2):
                load_stack(0, h, everything, [(stack_loaded[h], 16)])
            with sp.Fori(1, SB_UNITS) as v:
                for s in range(RAW):
                    load_granule(v * G_QKV + (RAW + s), s)
                staged(v)
                for h in range(2):
                    sp.wait_ge(scores_done, v * 16 + (8 * h - 8))
                    load_stack(v, h, everything, [(stack_loaded[h], 16)])
            for v in range(SB_UNITS, UNITS):
                for s in range(RAW):
                    load_granule(v * G_QKV + RAW + s, s)
                staged(v)
                for m in range(2):
                    sp.wait_ge(scores_done, v * 16 + (8 * m - 8))
                    if v == SB_UNITS:
                        load_stack(v, m, everything, [(stack_half[0], 32), (stack_half[1], 32)])
                    else:
                        for h in range(2):
                            load_stack(v, h, slice(m * HALF, (m + 1) * HALF), [(stack_half[m], 16)])
            first = (UNITS + 1) * G_QKV
            with sp.Fori(first // RAW, GRANULES // RAW) as it:
                for s in range(RAW):
                    load_granule(it * RAW + s, s)
            for s in range(GRANULES % RAW):
                load_granule(GRANULES // RAW * RAW + s, s)
            sp.wait_ge(halves_done, 2 * G_OUT0)
            sp.dma_start(post[:], norm_post.partition_broadcast(P)).then_inc(late_loaded, 16)
            for t in range(NT):
                sp.dma_start(x_again[:, t, :], x[t * P:(t + 1) * P, :]).then_inc(xr_loaded[t], 16)
            for t in range(NT):
                sp.wait_ge(fin_done, t + 1)
                sp.dma_start(out[t * P:(t + 1) * P, :], x_again[:, t, :]).then_inc(out_stored, 16)
            sp.wait_ge(out_stored, 16 * NT)

        @block.gpsimd
        def _(pool):
            pool.memset(zeros[:], 0.0).then_inc(consts, 1)
            pool.memset(ident[:], 0.0).then_inc(consts, 1)
            pool.wait_ge(consts, 2)
            pool.affine_select(out=ident[:], in_=ident[:], compare_op=ALU.not_equal, fill=1.0, base=0,
                               pattern=[[-1, P]], channel_multiplier=1).then_inc(consts, 1)
            pool.iota(alibi[:], pattern=[[-1, S]], base=0, channel_multiplier=1,
                      allow_small_or_imprecise_dtypes=True).then_inc(consts, 1)

            def split(g, s, wait_used):
                pool.wait_ge(raw_loaded[s], g_loads(g, s))
                if wait_used:
                    pool.wait_ge(halves_done, g * 2 + 2 * (1 - SPLIT))
                pool.tensor_tensor(whi[:, s % SPLIT, :], raw[:, s, :], zeros[:], ALU.add).then_inc(w_hi_done, 1)
                pool.wait_ge(w_hi_done, g + 1)
                pool.tensor_tensor(wlo[:, s % SPLIT, :], raw[:, s, :], f32(whi[:, s % SPLIT, :]),
                                   ALU.subtract).then_inc(w_ready, 1)

            loads = [16]

            def g_loads(g, s):
                return loads[0]

            for s in range(RAW):
                split(s, s, s >= SPLIT)
            with pool.Fori(1, GRANULES // RAW) as it:
                loads[0] = it * 16 + 16
                for s in range(RAW):
                    split(it * RAW + s, s, True)
            loads[0] = GRANULES // RAW * 16 + 16
            for s in range(GRANULES % RAW):
                split(GRANULES // RAW * RAW + s, s, True)
            for t in range(NT):
                pool.wait_ge(xr_loaded[t], 16)
                pool.wait_ge(y_scaled, t + 1)
                pool.tensor_tensor(x_again[:, t, HALF:], x_again[:, t, HALF:], merged[:, t, HALF:],
                                   ALU.add).then_inc(fin_done, 1)

        @block.tensor
        def _(pe):
            def three(ps, a_hi, a_lo, b_hi, b_lo, first, last):
                pe.matmul(ps, a_hi, b_hi, start=first, stop=False)
                pe.matmul(ps, a_hi, b_lo, start=False, stop=False)
                return pe.matmul(ps, a_lo, b_hi, start=False, stop=last)

            for half in range(2):
                pe.wait_ge(x_normed, 4 * half + 4)
                for k in range(KC):
                    if half == 0 and k == 0:
                        pe.wait_ge(consts, 3)
                    if half:
                        pe.wait_ge(hT_done, k + 1)
                    for t in range(4):
                        mm = pe.transpose(bank[:, k, t * P:(t + 1) * P],
                                          xt[:, 4 * half + t, k * P:(k + 1) * P], ident[:])
                    mm.then_inc(hT_ps_done, 1)
            pe.wait_ge(hT_done, 2 * KC)
            pe.sem_inc(av_done, 2)

            def w_tile(a, kk):
                return (whi[:, a, kk * P:(kk + 1) * P], wlo[:, a, kk * P:(kk + 1) * P])

            def project(g0, half0, c, skip_wait=False):
                _, a, n, pair = chunk_parts(c)
                if pair == 0:
                    if n == 0:
                        pe.wait_ge(w_ready, g0 + (a + 1))
                    if a == 0 and not skip_wait:
                        pe.wait_ge(proj_read, half0 + (n - 1))
                ps = proj_ps[:, n * HALF:(n + 1) * HALF]
                for kk in (2 * pair, 2 * pair + 1):
                    k = 4 * a + kk
                    hi, lo = w_tile(a, kk)
                    mm = three(ps, hi, lo, hT_hi[:, k, n * HALF:(n + 1) * HALF],
                               hT_lo[:, k, n * HALF:(n + 1) * HALF], k == 0, k == KC - 1)
                if pair == 1:
                    mm.then_inc(halves_done, 1)

            def project_chunk(v, c):
                b = c // 8
                if v is None:
                    project(G_Z0 + 2 * b, 6 * UNITS + 2 * b, c % 8)
                else:
                    project(v * G_QKV + 2 * b, v * 6 + 2 * b, c % 8,
                            skip_wait=isinstance(v, int) and v == 0 and b == 0)

            def transpose_v(un, n):
                pe.wait_ge(t_free, un.t(n + 1))
                if n == 0:
                    pe.wait_ge(proj_read, un.per(6, 6))
                for b in range(4):
                    j = 4 * n + b
                    mm = pe.transpose(t_ps[:, b * P:(b + 1) * P], vT[:, j * P:(j + 1) * P], ident[:])
                mm.then_inc(t_full, 1)

            def scores(un, n):
                h, i = (n // NT, n % NT) if un.sb else (n % 2, n // 2)
                free = sb_scores_read if un.sb else df_scores_read
                pe.wait_ge(free, un.i * 16 + (n + 1))
                if i == 0 and un.sb:
                    pe.wait_ge(stack_loaded[h], un.i * 64 + 64)
                if i == 0 and not un.sb:
                    for part in range(2):
                        pe.wait_ge(stack_half[part], un.i * 128 + 128)
                ps = score_ps[n % 2]
                for m, (c0, c1) in enumerate(score_columns(i)):
                    o = ps[:, c0:c1]
                    kk = stack[:, h, 2, c0:c1]
                    q1 = stack[:, h, 0, i * P:(i + 1) * P]
                    q2 = stack[:, h, 1, i * P:(i + 1) * P]
                    pe.matmul(o, q1, kk, start=True, stop=False)
                    if un.sb and m == 0:
                        mask = neg_mask[:, P:3 * P] if i % 2 == 0 else neg_mask[:, 0:2 * P]
                        pe.matmul(ps[:, c0:c0 + 2 * P], ident_r[:], mask, start=False, stop=False)
                    mm = pe.matmul(o, q2, kk, start=False, stop=True)
                mm.then_inc(scores_done, 1)

            def transpose_row(un, n, k):
                h, i = un.kind.slots[n]
                pe.wait_ge(t_free, un.t(un.kind.first_use[n] + k + 1))
                if k == 0:
                    pe.wait_ge(row_ready, un.w(n + 1))
                for b, j in enumerate(un.kind.uses[n][k]):
                    mm = pe.transpose(t_ps[:, b * P:(b + 1) * P], beta[n % 2][:, (j - i) * P:(j - i + 1) * P],
                                      ident[:])
                mm.then_inc(t_full, 1)

            def attend(un, grp):
                h, i0 = un.kind.slots[2 * grp]
                pe.wait_ge(t_free, un.t(un.kind.first_use[2 * grp + 1] + len(un.kind.uses[2 * grp + 1]) + 1))
                pe.wait_ge(o_saved, un.g(grp + 1))
                c0 = 64 * h
                for jr in range(NT - i0):
                    j = i0 + jr
                    mm = three(o_ps[:, 0:2 * P], v_hi[:, j, c0:c0 + P], v_lo[:, j, c0:c0 + P],
                               wT_hi[grp % 2][:, jr, :], wT_lo[grp % 2][:, jr, :], jr == 0, j == NT - 1)
                mm.then_inc(av_done, 1)

            def unit(un, nxt):
                ns = len(un.kind.slots)
                chunks = un.kind.chunks if nxt is not None else numbered(LAST_CHUNKS)
                transpose_v(un, 0)
                for n in range(2):
                    scores(un, n)
                transpose_v(un, 1)
                before = chunks[0]
                for c in before[:len(before) // 2]:
                    project_chunk(nxt, c)
                if not un.sb:
                    for c in range(2):
                        scores(un, 2 + c)
                for c in before[len(before) // 2:]:
                    project_chunk(nxt, c)
                for n in range(ns):
                    transpose_row(un, n, 0)
                    if un.sb and n + 2 < ns:
                        scores(un, n + 2)
                    for k in range(1, len(un.kind.uses[n])):
                        transpose_row(un, n, k)
                    if n >= 2 and n % 2 == 0:
                        attend(un, n // 2 - 1)
                    late = chunks[n + 1]
                    for c in late[:len(late) // 2]:
                        project_chunk(nxt, c)
                    if not un.sb and n + 2 < ns:
                        for c in range(2):
                            scores(un, 2 * (n + 2) + c)
                    for c in late[len(late) // 2:]:
                        project_chunk(nxt, c)
                attend(un, ns // 2 - 1)

            for c in range(24):
                project_chunk(0, c)
            pe.wait_ge(pads_done, 1)
            with pe.Fori(0, SB_UNITS) as i:
                unit(Unit(SB, i), i + 1)
            with pe.Fori(0, DF_UNITS - 1) as i:
                unit(Unit(DF, i), i + (SB_UNITS + 1))
            unit(Unit(DF, DF_UNITS - 1), None)

            def mean_square(j):
                for n in range(2):
                    pe.wait_ge(sq_split, j * 2 + (n + 1))
                    o = mean_ps[:, n * HALF:(n + 1) * HALF]
                    pe.matmul(o, mean_w[:], sq_hi[:], start=True, stop=False)
                    pe.matmul(o, mean_w[:], sq_lo[:], start=False, stop=True).then_inc(mean_done, 1)

            for c in range(sum(LAST_CHUNKS), 8 * SB_UNITS):
                project_chunk(None, c)
            with pe.Fori(0, DF_UNITS) as j:
                for c in range(8):
                    if c == 4:
                        mean_square(j)
                    project(j * 2 + (G_Z0 + 2 * SB_UNITS), j * 2 + (6 * UNITS + 2 * SB_UNITS), c)

            with pe.Fori(0, KC) as m:
                for b in range(2):
                    for a in range(2):
                        pe.wait_ge(w_ready, m * 6 + (G_FIN0 + 2 * b + a + 1))
                        for n in range(2):
                            if a == 0:
                                pe.wait_ge(gates_done, m * 4 + (2 * b + n + 1))
                            for kk in range(4):
                                k = 4 * a + kk
                                hi, lo = w_tile(a, kk)
                                mm = three(bank[:, 2 * b + n, :], hi, lo, hT_hi[:, k, n * HALF:(n + 1) * HALF],
                                           hT_lo[:, k, n * HALF:(n + 1) * HALF], k == 0, k == KC - 1)
                            mm.then_inc(halves_done, 1)
                for b in range(2):
                    pe.wait_ge(w_ready, m * 6 + (G_FIN0 + 4 + b + 1))
                    if b == 0:
                        pe.wait_ge(z_done, 2 * UNITS + 2)
                    for n in range(2):
                        pe.wait_ge(y_read, m * 4 + (2 * b + n + 1))
                        for kk in range(4):
                            hi, lo = w_tile(b, kk)
                            mm = three(bank[:, 4 + 2 * b + n, :], hi, lo,
                                       gated_hi[:, 4 * b + kk, n * HALF:(n + 1) * HALF],
                                       gated_lo[:, 4 * b + kk, n * HALF:(n + 1) * HALF], kk == 0, kk == 3)
                        mm.then_inc(halves_done, 1)

            for n in range(2):
                for k in range(KC):
                    g = G_OUT0 + n * KC + k
                    pe.wait_ge(w_ready, g + 1)
                    if n == 0:
                        pe.wait_ge(m_done, k + 1)
                    for t in range(NT):
                        if k == 0 and n == 0:
                            pe.wait_ge(*((gates_done, 4 * KC + 4) if t < 4 else (y_read, 4 * KC + 4)))
                        if k == 0 and n == 1:
                            pe.wait_ge(y_saved, t + 1)
                        mm = three(bank[:, t, :], hT_hi[:, k, t * P:(t + 1) * P], hT_lo[:, k, t * P:(t + 1) * P],
                                   whi[:, g % SPLIT, :], wlo[:, g % SPLIT, :], k == 0, k == KC - 1)
                        if k == KC - 1 and t < NT - 1:
                            mm.then_inc(out_ps, 1)
                        elif t == NT - 1:
                            mm.then_inc(halves_done, 2)

        @block.scalar
        def _(act):
            def copy(dst, src, scale=1.0):
                return act.activation(dst, src, ACT.Copy, scale=scale)

            act.sem_inc(sb_scores_read, 2)
            act.sem_inc(o_saved, 1)
            act.sem_inc(o_stored, 16)

            act.wait_ge(consts_fixed, 1)
            for half in range(2):
                for t in range(4 * half, 4 * half + 4):
                    act.wait_ge(x_loaded[t], 16)
                    if t:
                        act.wait_ge(sumsq_done, t)
                    act.activation(junk[:], xt[:, t, :], ACT.Square,
                                   accum_out=sumsq[:, t:t + 1]).then_inc(sumsq_done, 1)
                act.wait_ge(sumsq_done, 4 * half + 4)
                act.activation(std[:, 4 * half:4 * half + 4], sumsq[:, 4 * half:4 * half + 4], ACT.Sqrt,
                               bias=eps_col, scale=1.0 / D).then_inc(std_done, 1)
            act.wait_ge(const_loaded, 48)
            for q in range(2 * KC):
                half, k = q // KC, q % KC
                act.wait_ge(hT_ps_done, q + 1)
                act.activation(hT_hi[:, k, half * HALF:(half + 1) * HALF], bank[:, k, :], ACT.Copy,
                               scale=gain_pre[:, k:k + 1]).then_inc(hT_hi_done, 1)
            act.wait_ge(lam_step, 2)
            act.activation(lam_exp, lam_dot, ACT.Exp).then_inc(lam_exp_done, 1)

            def stage(v, c):
                b, _, n, _ = chunk_parts(c)
                if v is None or b == 2 or not completes(c):
                    return
                act.wait_ge(halves_done, v * (2 * G_QKV) + (2 * (2 * b + 1) + n + 1))
                if b == 0 and n == 0:
                    stage_is_free(v)
                copy(stage_hi[:, b, n * HALF:(n + 1) * HALF], proj_ps[:, n * HALF:(n + 1) * HALF],
                     HD ** -0.5 if b == 0 else 1.0).then_inc(stage_hi_done, 1)

            def stage_is_free(v):
                if isinstance(v, int) and v == 0:
                    return
                if loop_kind[0] is SB:
                    for h in range(2):
                        act.wait_ge(stack_loaded[h], v * 64)
                else:
                    for part in range(2):
                        act.wait_ge(stack_half[part], v * 128 - 128 * SB_UNITS)

            loop_kind = [SB]

            def t_hi(un, n, k):
                kind = un.kind
                h, i = kind.slots[n]
                grp = n // 2
                i0 = kind.slots[2 * grp][1]
                blocks = kind.uses[n][k]
                act.wait_ge(t_full, un.t(kind.first_use[n] + k + 1))
                if n % 2 == 0 and k == 0:
                    act.wait_ge(av_done, un.g(grp + 1))
                j0 = blocks[0] - i0
                copy(wT_hi[grp % 2][:, j0:j0 + len(blocks), (n % 2) * P:(n % 2 + 1) * P],
                     t_ps[:, 0:len(blocks) * P].rearrange("p (j c) -> p j c", c=P)).then_inc(t_hi_done, 1)

            def v_hi_part(un, n):
                act.wait_ge(t_full, un.t(n + 1))
                if n == 0:
                    act.wait_ge(av_done, un.g(2))
                dst = v_hi[:, 4 * n:4 * n + 4, :]
                if un.sb:
                    src = t_ps[:].rearrange("p (j a c) -> p j a c", j=4, a=2)
                    copy(dst.rearrange("p j (a c) -> p j a c", a=3)[:, :, 0:3:2, :], src).then_inc(t_hi_done, 1)
                else:
                    copy(dst[:, :, 0:P], t_ps[:].rearrange("p (j c) -> p j c", j=4)).then_inc(t_hi_done, 1)

            def save_o(un, grp):
                h, i0 = un.kind.slots[2 * grp]
                act.wait_ge(av_done, un.g(grp + 3))
                if grp == 0:
                    act.wait_ge(o_stored, un.per(16, 16))
                rows = slice(64 * h, 64 * h + 64) if un.sb else slice(0, P)
                cols = slice(i0 * P, (i0 + 2) * P)
                copy(o_sb[rows, cols], o_ps[rows, 0:2 * P]).then_inc(o_saved, 1)

            def sb_sigmoid(un, n, which):
                h, i = un.kind.slots[n]
                width = S - i * P
                if which == 0:
                    act.wait_ge(scores_done, un.per(16, n + 1))
                    act.wait_ge(t_full, un.t(un.kind.first_use[n - 2] + len(un.kind.uses[n - 2]) if n >= 2 else 1))
                    act.activation(keep[n % 2][:, 1:1 + width], score_ps[n % 2][:, i * P:S], ACT.Sigmoid,
                                   scale=-1.0).then_inc(keep_done, 1)
                else:
                    act.activation(beta[n % 2][:, 0:width], score_ps[n % 2][:, i * P:S],
                                   ACT.Sigmoid).then_inc(sb_scores_read, 1)

            def df_exp(un, n, c):
                h, i = un.kind.slots[n]
                width = S - i * P
                row = (beta, keep)[c][n % 2][:, 0:width]
                act.wait_ge(negmax_done, un.i * 16 + (2 * n + c + 1))
                act.activation(row, row, ACT.Exp, bias=stats[:, n % 2, 2 + c:3 + c],
                               accum_out=stats[:, n % 2, 4 + c:5 + c]).then_inc(exp_done, 1)

            def unit(un, nxt):
                ns = len(un.kind.slots)
                chunks = un.kind.chunks if nxt is not None else numbered(LAST_CHUNKS)
                loop_kind[0] = un.kind
                v_hi_part(un, 0)
                if un.sb:
                    sb_sigmoid(un, 0, 0)
                v_hi_part(un, 1)
                if un.sb:
                    sb_sigmoid(un, 0, 1)
                else:
                    df_exp(un, 0, 0)
                    df_exp(un, 0, 1)
                for n in range(ns):
                    more = n + 1 < ns
                    if more and un.sb:
                        sb_sigmoid(un, n + 1, 0)
                    t_hi(un, n, 0)
                    if more:
                        if un.sb:
                            sb_sigmoid(un, n + 1, 1)
                        else:
                            df_exp(un, n + 1, 0)
                    for k in range(1, len(un.kind.uses[n])):
                        t_hi(un, n, k)
                    if more and not un.sb:
                        df_exp(un, n + 1, 1)
                    if n >= 2 and n % 2 == 0:
                        save_o(un, n // 2 - 1)
                    for c in chunks[n]:
                        stage(nxt, c)
                for c in chunks[ns]:
                    stage(nxt, c)
                save_o(un, ns // 2 - 1)
                act.wait_ge(o_saved, un.g(ns // 2 + 1))
                act.dma_start(o_dram[un.u], o_sb[:]).then_inc(o_stored, 16)

            for c in range(24):
                stage(0, c)
            with act.Fori(0, SB_UNITS) as i:
                unit(Unit(SB, i), i + 1)
            with act.Fori(0, DF_UNITS - 1) as i:
                unit(Unit(DF, i), i + (SB_UNITS + 1))
            unit(Unit(DF, DF_UNITS - 1), None)

            act.wait_ge(o_stored, 16 * UNITS + 16)

            def load_o(v, b):
                act.dma_start(o_in[b][:], o_dram[v]).then_inc(o_loaded[b], 16)

            def z_sigmoid(v, n, src):
                act.wait_ge(z_done, v * 2 + (n + 1))
                act.sem_inc(waited, 1)
                act.activation(silu[:, n, :], src, ACT.Sigmoid).then_inc(z_sig, 1)

            def z_hi_part(v, n):
                act.wait_ge(z_gated, v * 2 + (n + 1))
                act.sem_inc(waited, 1)
                copy(gated_hi[:, v, n * HALF:(n + 1) * HALF], silu[:, n, :]).then_inc(z_hi, 1)

            def squares(j, b):
                act.wait_ge(o_loaded[b], 16 * (SB_UNITS // 2 + 1 + j // 2))
                for n in range(2):
                    if n:
                        act.wait_ge(sq_split, j * 2 + n)
                    act.activation(sq[:], o_in[b][:, n * HALF:(n + 1) * HALF], ACT.Square).then_inc(sq_done, 1)
                    act.wait_ge(sq_done, j * 2 + (n + 1))
                    if n:
                        act.wait_ge(mean_done, j * 2 + n)
                    copy(sq_hi[:], sq[:]).then_inc(sq_hi_done, 1)
                for n in range(2):
                    act.wait_ge(mean_done, j * 2 + (n + 1))
                    act.activation(rms[:, n * HALF:(n + 1) * HALF], mean_ps[:, n * HALF:(n + 1) * HALF],
                                   ACT.Ln, bias=eps_col).then_inc(rms_ln, 1)
                for n in range(2):
                    act.wait_ge(rms_ln, j * 2 + (n + 1))
                    half = rms[:, n * HALF:(n + 1) * HALF]
                    act.activation(half, half, ACT.Exp, scale=-0.5).then_inc(rms_done, 1)

            for b in range(2):
                load_o(b, b)
            act.wait_ge(early_z_done, 1)
            with act.Fori(0, SB_UNITS // 2) as i:
                for b in range(2):
                    v = i * 2 + b
                    for n in range(2):
                        z_sigmoid(v, n, early_z[:, v, n * HALF:(n + 1) * HALF])
                    for n in range(2):
                        z_hi_part(v, n)
                    load_o(v + 2, b)
            for j in range(DF_UNITS):
                v, b = j + SB_UNITS, j % 2
                squares(j, b)
                for n in range(2):
                    act.wait_ge(halves_done, v * 4 + (2 * G_Z0 + 2 + n + 1))
                    z_sigmoid(v, n, proj_ps[:, n * HALF:(n + 1) * HALF])
                for n in range(2):
                    z_hi_part(v, n)
                if v + 2 < UNITS:
                    load_o(v + 2, b)

            act.sem_inc(gates_done, 4)
            with act.Fori(0, KC) as m:
                for b in range(2):
                    for n in range(2):
                        q = 2 * b + n
                        act.wait_ge(halves_done, m * 12 + (2 * (G_FIN0 + 2 * b + 1) + n + 1))
                        act.wait_ge(merged_done, m * 2 + 2)
                        act.sem_inc(waited, 1)
                        act.activation(gate[:, q, :], bank[:, q, :], ACT.Sigmoid,
                                       bias=bias_gate[:, bass.ds(m + b * KC, 1)]).then_inc(gates_done, 1)

            for k in range(KC):
                act.wait_ge(merged_done, 2 * (k + 1) + 2)
                copy(hT_hi[:, k, :], merged[:, k, :]).then_inc(m_hi_done, 1)
            for t in range(NT):
                act.wait_ge(y_saved, t + 1)
                if t:
                    act.wait_ge(sq_half[0], t)
                act.activation(junk2[:], merged[:, t, 0:HALF], ACT.Square,
                               accum_out=sumsq[:, t:t + 1]).then_inc(sq_half[0], 1)
            for grp in range(2):
                for t in range(4 * grp, 4 * grp + 4):
                    if t < NT - 1:
                        act.wait_ge(out_ps, (NT - 1) + t + 1)
                    else:
                        act.wait_ge(halves_done, 2 * GRANULES)
                    if t:
                        act.wait_ge(sq_half[1], t)
                    else:
                        act.wait_ge(sq_half[0], NT)
                    act.activation(junk2[:], bank[:, t, :], ACT.Square,
                                   accum_out=std[:, t:t + 1]).then_inc(sq_half[1], 1)
                act.wait_ge(fin_step, 2 * grp + 1)
                cols = slice(4 * grp, 4 * grp + 4)
                act.activation(std[:, cols], sumsq[:, cols], ACT.Sqrt, bias=eps_col, scale=1.0 / D)\
                   .then_inc(y_std, 1)

        @block.vector
        def _(dve):
            dve.memset(eps_col, EPS).then_inc(consts_fixed, 1)
            dve.wait_ge(consts, 4)
            dve.tensor_copy(ident_r[:], ident[:])
            dve.memset(f32(neg_mask[:]), 0.0).then_inc(consts_fixed, 1)
            dve.scalar_tensor_tensor(alibi[:], alibi[:], -1.0, alibi[:], ALU.mult, ALU.min).then_inc(consts_fixed, 1)
            dve.tensor_tensor_scan(vT[:, 0:P], ident[:], zeros[:, 0:P], 0.0, ALU.add, ALU.add)\
               .then_inc(consts_fixed, 1)
            dve.wait_ge(consts_fixed, 4)
            dve.tensor_scalar(alibi[:], alibi[:], 0.25, None, ALU.mult).then_inc(consts_fixed, 1)
            dve.tensor_tensor(vT[:, P:2 * P], vT[:, 0:P], ident[:], ALU.subtract).then_inc(consts_fixed, 1)
            dve.wait_ge(consts_fixed, 6)
            dve.memset(alibi[64:128, 0:64], -3e38).then_inc(consts_fixed, 1)
            dve.tensor_scalar(neg_mask[:, P:2 * P], vT[:, P:2 * P], -NEG, NEG, ALU.mult, ALU.add)\
               .then_inc(consts_fixed, 1)
            dve.wait_ge(consts_fixed, 8)
            dve.sem_inc(t_free, 1)

            for half in range(2):
                cols = slice(4 * half, 4 * half + 4)
                dve.wait_ge(std_done, half + 1)
                dve.reciprocal(rstd[:, cols], std[:, cols]).then_inc(rstd_done, 1)
                dve.wait_ge(rstd_done, half + 1)
                for t in range(4 * half, 4 * half + 4):
                    dve.tensor_scalar(xt[:, t, :], xt[:, t, :], rstd[:, t:t + 1], None, ALU.mult)\
                       .then_inc(x_normed, 1)
            dve.wait_ge(lam_loaded, 32)
            dve.tensor_tensor(lam_in[:, 0], lam_in[:, 0], lam_in[:, 1], ALU.mult).then_inc(lam_step, 1)
            dve.wait_ge(lam_step, 1)
            dve.tensor_reduce(lam_dot, lam_in[:, 0], AX.X, ALU.add).then_inc(lam_step, 1)
            dve.wait_ge(const_loaded, 48)
            for q in range(2 * KC):
                half, k = q // KC, q % KC
                cols = slice(half * HALF, (half + 1) * HALF)
                dve.wait_ge(hT_hi_done, q + 1)
                dve.scalar_tensor_tensor(hT_lo[:, k, cols], bank[:, k, :], gain_pre[:, k:k + 1],
                                         f32(hT_hi[:, k, cols]), ALU.mult, ALU.subtract).then_inc(hT_done, 1)
            dve.wait_ge(lam_exp_done, 1)
            dve.tensor_tensor(neg_lam, lam_exp[:, 1:2], lam_exp[:, 0:1], ALU.subtract).then_inc(lam_step, 1)
            dve.wait_ge(lam_step, 3)
            dve.tensor_scalar(neg_lam, neg_lam, -LAMBDA_INIT, None, ALU.add).then_inc(lam_step, 1)
            dve.tensor_scalar(gain_head[:], gain_head[:], 1.0 - LAMBDA_INIT, None, ALU.mult).then_inc(lam_step, 1)
            for b in range(2):
                dve.memset(f32(wT_hi[b][:, 0, P:2 * P]), 0.0)
                dve.memset(f32(wT_lo[b][:, 0, P:2 * P]), 0.0)
                dve.memset(keep[b][:, 0:1], 1.0)
            dve.memset(f32(v_hi[:, :, 64:128]), 0.0)
            dve.memset(f32(v_lo[:, :, 64:128]), 0.0).then_inc(pads_done, 1)

            def stage(v, c):
                b, _, n, _ = chunk_parts(c)
                if not completes(c):
                    return
                cols = slice(n * HALF, (n + 1) * HALF)
                ps = proj_ps[:, cols]
                if v is None:
                    dve.wait_ge(halves_done, 2 * (G_Z0 + 2 * b + 1) + n + 1)
                    if b == 0 and n == 0:
                        for part in range(2):
                            dve.wait_ge(stack_half[part], 128 * DF_UNITS)
                    dve.tensor_copy(early_z[:, b, cols], ps).then_inc(proj_read, 1)
                elif b == 2:
                    dve.wait_ge(halves_done, v * (2 * G_QKV) + (2 * (2 * b + 1) + n + 1))
                    dve.tensor_copy(vT[:, cols], ps).then_inc(proj_read, 1)
                else:
                    dve.wait_ge(stage_hi_done, v * 4 + (2 * b + n + 1))
                    if b == 0:
                        dve.scalar_tensor_tensor(stage_lo[:, b, cols], ps, HD ** -0.5, f32(stage_hi[:, b, cols]),
                                                 ALU.mult, ALU.subtract).then_inc(proj_read, 1)
                    else:
                        dve.tensor_tensor(stage_lo[:, b, cols], ps, f32(stage_hi[:, b, cols]),
                                          ALU.subtract).then_inc(proj_read, 1)

            def t_lo(un, n, k):
                kind = un.kind
                grp = n // 2
                i0 = kind.slots[2 * grp][1]
                blocks = kind.uses[n][k]
                dve.wait_ge(t_hi_done, un.t(kind.first_use[n] + k + 1))
                j0 = blocks[0] - i0
                cols = slice((n % 2) * P, (n % 2 + 1) * P)
                dve.tensor_tensor(wT_lo[grp % 2][:, j0:j0 + len(blocks), cols],
                                  t_ps[:, 0:len(blocks) * P].rearrange("p (j c) -> p j c", c=P),
                                  f32(wT_hi[grp % 2][:, j0:j0 + len(blocks), cols]),
                                  ALU.subtract).then_inc(t_free, 1)

            def v_lo_part(un, n):
                dve.wait_ge(t_hi_done, un.t(n + 1))
                rows = slice(4 * n, 4 * n + 4)
                if un.sb:
                    view = lambda t: t[:, rows, :].rearrange("p j (a c) -> p j a c", a=3)[:, :, 0:3:2, :]
                    src = t_ps[:].rearrange("p (j a c) -> p j a c", j=4, a=2)
                else:
                    view = lambda t: t[:, rows, 0:P]
                    src = t_ps[:].rearrange("p (j c) -> p j c", j=4)
                dve.tensor_tensor(view(v_lo), src, f32(view(v_hi)), ALU.subtract).then_inc(t_free, 1)

            def sb_scan(un, n):
                i = un.kind.slots[n][1]
                width = S - i * P
                k = keep[n % 2][:, 1:1 + width]
                dve.wait_ge(keep_done, un.per(16, n + 1))
                dve.tensor_tensor_scan(k, k, zeros[:, 0:1].to_broadcast([P, width]), 1.0,
                                       ALU.mult, ALU.add).then_inc(scan_done, 1)

            def sb_weights(un, n):
                i = un.kind.slots[n][1]
                width = S - i * P
                dve.wait_ge(sb_scores_read, un.per(16, n + 3))
                dve.wait_ge(scan_done, un.per(16, n + 1))
                dve.tensor_tensor(beta[n % 2][:, 0:width], beta[n % 2][:, 0:width], keep[n % 2][:, 0:width],
                                  ALU.mult).then_inc(row_ready, 1)

            def df_logits(un, n, c):
                i = un.kind.slots[n][1]
                width = S - i * P
                st = stats[:, n % 2]
                if c == 0:
                    dve.wait_ge(t_full, un.t(un.kind.first_use[n - 2] + len(un.kind.uses[n - 2]) if n >= 2 else 1))
                dve.wait_ge(scores_done, un.per(16, 2 * n + c + 1))
                dve.sem_inc(waited, 1)
                dve.tensor_tensor_reduce(out=(beta, keep)[c][n % 2][:, 0:width], in0=score_ps[c][:, i * P:S],
                                         in1=alibi[:, 0:width], scale=1.0, scalar=-3.4e38, op0=ALU.add,
                                         op1=ALU.max, accum_out=st[:, c:c + 1]).then_inc(df_scores_read, 1)
                dve.wait_ge(df_scores_read, un.i * 16 + (2 * n + c + 3))
                dve.tensor_scalar(st[:, 2 + c:3 + c], st[:, c:c + 1], -1.0, None, ALU.mult).then_inc(negmax_done, 1)

            def df_weights(un, n):
                i = un.kind.slots[n][1]
                width = S - i * P
                st = stats[:, n % 2]
                p1, p2 = beta[n % 2][:, 0:width], keep[n % 2][:, 0:width]
                dve.wait_ge(exp_done, un.i * 16 + (2 * n + 2))
                dve.reciprocal(st[:, 6:8], st[:, 4:6]).then_inc(recip_done, 1)
                dve.wait_ge(recip_done, un.i * NT + (n + 1))
                dve.tensor_scalar(st[:, 8:9], st[:, 7:8], neg_lam, None, ALU.mult).then_inc(scaled, 1)
                dve.tensor_scalar(p1, p1, st[:, 6:7], None, ALU.mult).then_inc(scaled, 1)
                dve.wait_ge(scaled, un.i * 16 + (2 * n + 2))
                dve.scalar_tensor_tensor(p1, p2, st[:, 8:9], p1, ALU.mult, ALU.add).then_inc(row_ready, 1)

            def unit(un, nxt):
                ns = len(un.kind.slots)
                chunks = un.kind.chunks if nxt is not None else numbered(LAST_CHUNKS)
                v_lo_part(un, 0)
                if un.sb:
                    sb_scan(un, 0)
                    v_lo_part(un, 1)
                    sb_weights(un, 0)
                else:
                    df_logits(un, 0, 0)
                    v_lo_part(un, 1)
                    df_logits(un, 0, 1)
                    df_weights(un, 0)
                for n in range(ns):
                    more = n + 1 < ns
                    if more:
                        if un.sb:
                            sb_scan(un, n + 1)
                        else:
                            df_logits(un, n + 1, 0)
                    t_lo(un, n, 0)
                    if more:
                        if un.sb:
                            sb_weights(un, n + 1)
                        else:
                            df_logits(un, n + 1, 1)
                    for k in range(1, len(un.kind.uses[n])):
                        t_lo(un, n, k)
                    for c in chunks[n]:
                        stage(nxt, c)
                    if more and not un.sb:
                        df_weights(un, n + 1)
                for c in chunks[ns]:
                    stage(nxt, c)

            for c in range(24):
                stage(0, c)
            with dve.Fori(0, SB_UNITS) as i:
                unit(Unit(SB, i), i + 1)
            dve.sem_inc(df_scores_read, 2)
            with dve.Fori(0, DF_UNITS - 1) as i:
                unit(Unit(DF, i), i + (SB_UNITS + 1))
                dve.tensor_scalar(alibi[:], alibi[:], 0.25, None, ALU.mult).then_inc(consts_fixed, 1)
                dve.wait_ge(consts_fixed, i + 9)
            unit(Unit(DF, DF_UNITS - 1), None)

            for c in range(sum(LAST_CHUNKS), 8 * SB_UNITS):
                stage(None, c)

            dve.wait_ge(proj_read, 6 * UNITS + 2 * SB_UNITS)
            dve.sem_inc(early_z_done, 1)
            dve.wait_ge(o_stored, 16 * UNITS + 16)
            dve.memset(f32(mean_w[:]), 1.0 / P)
            dve.sem_inc(z_done, 2)

            def z_half(v, n, b, z, step, ready):
                dve.wait_ge(z_sig, v * 2 + (n + 1))
                dve.tensor_tensor(silu[:, n, :], z, silu[:, n, :], ALU.mult).then_inc(step, 1)
                dve.wait_ge(step, ready)
                dve.tensor_tensor(silu[:, n, :], silu[:, n, :], o_in[b][:, n * HALF:(n + 1) * HALF],
                                  ALU.mult).then_inc(z_gated, 1)

            def z_lo_part(v, n):
                cols = slice(n * HALF, (n + 1) * HALF)
                dve.wait_ge(z_hi, v * 2 + (n + 1))
                dve.tensor_tensor(gated_lo[:, v, cols], silu[:, n, :], f32(gated_hi[:, v, cols]),
                                  ALU.subtract).then_inc(z_done, 1)

            with dve.Fori(0, SB_UNITS // 2) as i:
                for b in range(2):
                    v = i * 2 + b
                    dve.wait_ge(o_loaded[b], i * 16 + 16)
                    for n in range(2):
                        z_half(v, n, b, early_z[:, v, n * HALF:(n + 1) * HALF], z_silu, v * 2 + (n + 1))
                    for n in range(2):
                        z_lo_part(v, n)
            for j in range(DF_UNITS):
                v, b = j + SB_UNITS, j % 2
                for n in range(2):
                    dve.wait_ge(sq_hi_done, j * 2 + (n + 1))
                    dve.tensor_tensor(sq_lo[:], sq[:], f32(sq_hi[:]), ALU.subtract).then_inc(sq_split, 1)
                for n in range(2):
                    cols = slice(n * HALF, (n + 1) * HALF)
                    dve.wait_ge(rms_done, j * 2 + (n + 1))
                    dve.scalar_tensor_tensor(o_in[b][:, cols], o_in[b][:, cols], gain_head[:, 0:1], rms[:, cols],
                                             ALU.mult, ALU.mult).then_inc(normed, 1)
                for n in range(2):
                    dve.wait_ge(normed, j * 2 + (n + 1))
                    z_half(v, n, b, proj_ps[:, n * HALF:(n + 1) * HALF], proj_read,
                           v * 2 + (6 * UNITS + n + 1))
                for n in range(2):
                    z_lo_part(v, n)

            dve.sem_inc(y_read, 4)
            dve.sem_inc(merged_done, 2)
            def merge(m):
                for b in range(2):
                    for n in range(2):
                        q = 2 * b + n
                        cols = slice(n * HALF, (n + 1) * HALF)
                        dve.wait_ge(halves_done, m * 12 + (2 * (G_FIN0 + 4 + b) + n + 1))
                        if q == 0:
                            dve.wait_ge(gates_done, m * 4 + 8)
                        dst = merged[:, m, cols] if b == 0 else gate[:, q, :]
                        dve.tensor_tensor(dst, bank[:, 4 + q, :], gate[:, q, :], ALU.mult).then_inc(y_read, 1)
                for n in range(2):
                    cols = slice(n * HALF, (n + 1) * HALF)
                    dve.wait_ge(y_read, m * 4 + (n + 7))
                    dve.tensor_tensor(merged[:, m, cols], merged[:, m, cols], gate[:, 2 + n, :],
                                      ALU.add).then_inc(merged_done, 1)

            def merged_lo(k):
                dve.wait_ge(m_hi_done, k + 1)
                dve.tensor_tensor(hT_lo[:, k, :], merged[:, k, :], f32(hT_hi[:, k, :]), ALU.subtract)\
                   .then_inc(m_done, 1)

            with dve.Fori(0, KC - 1) as m:
                merge(m)
            for k in range(KC - 1):
                merged_lo(k)
            merge(KC - 1)
            merged_lo(KC - 1)
            dve.wait_ge(m_done, KC)
            for t in range(NT):
                if t < NT - 1:
                    dve.wait_ge(out_ps, t + 1)
                else:
                    dve.wait_ge(halves_done, 2 * (G_OUT0 + KC))
                dve.tensor_copy(merged[:, t, 0:HALF], bank[:, t, :]).then_inc(y_saved, 1)
            dve.wait_ge(late_loaded, 16)
            for t in range(NT):
                dve.wait_ge(sq_half[0], t + 1)
                dve.tensor_tensor(merged[:, t, 0:HALF], merged[:, t, 0:HALF], post[:, 0:HALF], ALU.mult)\
                   .then_inc(y_post, 1)
            for grp in range(2):
                cols = slice(4 * grp, 4 * grp + 4)
                dve.wait_ge(sq_half[1], 4 * grp + 4)
                dve.tensor_tensor(sumsq[:, cols], sumsq[:, cols], std[:, cols], ALU.add).then_inc(fin_step, 1)
                dve.wait_ge(y_std, grp + 1)
                dve.reciprocal(rstd[:, cols], std[:, cols]).then_inc(fin_step, 1)
                dve.wait_ge(fin_step, 2 * grp + 2)
                for t in range(4 * grp, 4 * grp + 4):
                    dve.wait_ge(y_post, t + 1)
                    dve.wait_ge(xr_loaded[t], 16)
                    dve.scalar_tensor_tensor(x_again[:, t, 0:HALF], merged[:, t, 0:HALF], rstd[:, t:t + 1],
                                             x_again[:, t, 0:HALF], ALU.mult, ALU.add)
                    dve.scalar_tensor_tensor(merged[:, t, HALF:], bank[:, t, :], rstd[:, t:t + 1], post[:, HALF:],
                                             ALU.mult, ALU.mult).then_inc(y_scaled, 1)


def granules(w_in, w_gate, w_sb, w_df, w_out):
    import numpy as np

    def columns(w, c):
        part = w[:, c:c + P].reshape(-1, 4, P, P)
        return part.transpose(0, 2, 1, 3).reshape(-1, P, HALF)

    def column(u, part):
        return (u // 4) * 2048 + part * 512 + (u % 4) * P

    g = [columns(w_in, column(u, part)) for u in range(UNITS) for part in range(3)]
    g += [columns(w_in, column(u, 3)) for u in range(UNITS)]
    for m in range(KC):
        g += [columns(w_gate, m * P), columns(w_gate, D + m * P), columns(w_sb, m * P), columns(w_df, m * P)]
    g += [w_out[k * P:(k + 1) * P, n * HALF:(n + 1) * HALF][None] for n in range(2) for k in range(KC)]
    return np.ascontiguousarray(np.concatenate(g, axis=0))


def kernel(x, norm_pre, norm_post, w_in, w_gate, b_gate, w_branch_sb, w_branch_df, w_out, lambda_q, lambda_k,
           df_head_norm):
    import numpy as np
    import concourse.bacc as bacc
    from concourse.bass_utils import run_bass_kernel_spmd

    a = {n: np.asarray(v) for n, v in dict(
        x=x, norm_pre=norm_pre, norm_post=norm_post, w_in=w_in, w_gate=w_gate, b_gate=b_gate, w_sb=w_branch_sb,
        w_df=w_branch_df, w_out=w_out, lambda_q=lambda_q, lambda_k=lambda_k, head_norm=df_head_norm).items()}
    cont = np.ascontiguousarray
    ins = {
        "x_rev": cont(a["x"][0, ::-1]),
        "w_all": granules(a["w_in"][0], a["w_gate"][0], a["w_sb"][0], a["w_df"][0], a["w_out"][0]),
        "norm_pre_t": cont(a["norm_pre"][0].reshape(KC, P).T),
        "norm_post_r": cont(a["norm_post"][0]),
        "b_gate_t": cont(a["b_gate"][0].reshape(2 * KC, P).T),
        "lambda_q_r": cont(a["lambda_q"][0]),
        "lambda_k_r": cont(a["lambda_k"][0]),
        "head_norm_t": cont(a["head_norm"][0].reshape(P, 1)),
    }
    nc = bacc.Bacc("TRN2", target_bir_lowering=False, num_devices=1)
    args = [nc.dram_tensor(n, v.shape, mybir.dt.from_np(v.dtype), kind="ExternalInput").ap() for n, v in ins.items()]
    out = nc.dram_tensor("out_rev", (S, D), F32, kind="ExternalOutput").ap()
    o_dram = nc.dram_tensor("o_scratch", (UNITS, P, S), F32, kind="Internal").ap()
    xx, w_all, npre, npost, bg, lq, lk, hn = args
    build(nc, xx, w_all, npre, npost, bg, lq, lk, hn, out, o_dram)
    r = run_bass_kernel_spmd(nc, [ins], core_ids=[0])
    return r.results[0]["out_rev"][::-1].reshape(1, S, D)
```

```python
from contextlib import ExitStack

import concourse.bass as bass
from concourse import mybir

F32 = mybir.dt.float32
F32R = mybir.dt.float32r
ALU = mybir.AluOpType
ACT = mybir.ActivationFunctionType
AX = mybir.AxisListType

P = 128
S = 1024
D = 1024
KC = D // P
NT = S // P
HALF = 512
HD = 64
EPS = 1e-6
LAMBDA_INIT = 0.8 - 0.6 * 1.0
SB_UNITS, DF_UNITS = 4, 4
UNITS = SB_UNITS + DF_UNITS
G_QKV = 6
G_Z0 = UNITS * G_QKV
G_FIN0 = G_Z0 + 2 * UNITS
G_OUT0 = G_FIN0 + 6 * KC
G_LAST0 = G_OUT0 + KC
GRANULES = G_OUT0 + 2 * KC
Z_ORDER = list(range(SB_UNITS, UNITS)) + list(range(SB_UNITS))
RAW = 6
SPLIT = 2
ROWS = 3

SB_SLOTS = [(h, i) for h in range(2) for i in range(NT)]
DF_SLOTS = [(0, i) for i in range(NT)]
SB_PLAN = dict(ahead=2,
               pe=["chunks 0", "transposes", "chunks 1", "attend", "scores", "more transposes", "chunks 2"],
               act=["row a", "hi", "stage", "row b", "output", "more hi"],
               dve=["row a", "lo", "stage", "row b", "more lo", "output"],
               chunks=[(2, 1, 1), (0, 1, 1), (0, 2, 0), (1, 0, 0), (1, 1, 0), (1, 0, 0), (0, 0, 0),
                       (0, 0, 0), (1, 1, 0), (0, 1, 0), (1, 1, 0), (1, 0, 0), (1, 1, 1), (0, 0, 0),
                       (0, 0, 1), (0, 0, 0), (1, 1, 0)])
DF_PLAN = dict(ahead=1,
               pe=["chunks 0", "transposes", "attend", "chunks 1", "chunks 2", "more transposes", "scores"],
               act=["stage", "row a", "hi", "row b", "more hi", "output"],
               dve=["row a", "row b", "stage", "lo", "weights", "more lo"],
               chunks=[(2, 4, 2), (0, 1, 1), (1, 1, 2), (0, 0, 0), (1, 1, 1), (1, 0, 0), (1, 0, 0),
                       (3, 0, 1), (0, 0, 1)])
LAST_PLAN = dict(ahead=1,
                 pe=["transposes", "attend", "chunks 0", "chunks 1", "more transposes", "chunks 2", "scores"],
                 act=["hi", "row a", "row b", "output", "more hi", "stage"],
                 dve=["stage", "row a", "row b", "lo", "weights", "more lo"],
                 chunks=[(3, 4, 3), (2, 0, 1), (0, 3, 0), (1, 0, 1), (2, 0, 1), (0, 0, 2), (0, 1, 4),
                         (0, 1, 0), (0, 0, 3)])


def rows_of(plan, n):
    if plan["ahead"] == 1:
        return [n + 1]
    return [1, 2] if n == 0 else [n + 2]


def transposes_of(slots):
    out = []
    for _, i in slots:
        blocks = list(range(i, NT))
        out.append([blocks[a:a + 4] for a in range(0, len(blocks), 4)])
    return out


def chunk_parts(c):
    return c // 8, (c % 8) // 4, (c % 4) // 2, c % 2


def completes(c):
    return c % 8 in (5, 7)


def numbered(plan):
    out, at = [], 0
    for counts in plan:
        parts = []
        for c in counts:
            parts.append(list(range(at, at + c)))
            at += c
        out.append(parts)
    return out


def plan_of(un, nxt):
    return LAST_PLAN if nxt is None else un.kind.plan


class Kind:

    def __init__(self, name, slots, plan):
        self.name, self.slots = name, slots
        self.uses = transposes_of(slots)
        self.first_use = []
        n = 2
        for u in self.uses:
            self.first_use.append(n)
            n += len(u)
        self.per_t = n
        self.per_w = len(slots)
        self.per_g = len(slots) // 2
        self.plan = plan


SB = Kind("sb", SB_SLOTS, SB_PLAN)
DF = Kind("df", DF_SLOTS, DF_PLAN)


class Unit:

    def __init__(self, kind, i):
        self.kind, self.i = kind, i
        sb = kind is SB
        self.sb = sb
        self.u = i if sb else i + SB_UNITS
        self.base_t = (0 if sb else SB_UNITS * SB.per_t)
        self.base_w = (0 if sb else SB_UNITS * SB.per_w)
        self.base_g = (0 if sb else SB_UNITS * SB.per_g)

    def t(self, n):
        return self.i * self.kind.per_t + (self.base_t + n)

    def w(self, n):
        return self.i * self.kind.per_w + (self.base_w + n)

    def g(self, n):
        return self.i * self.kind.per_g + (self.base_g + n)

    def row_free(self, n):
        back = n - ROWS
        return self.t(self.kind.first_use[back] + len(self.kind.uses[back]) if back >= 0 else 1)

    def per(self, count, n):
        return self.u * count + n


def build(nc, x, w_all, norm_pre, norm_post, b_gate, lam_q, lam_k, head_norm, out, o_dram):
    ctx = ExitStack()
    with ctx:
        def sbuf(name, shape, dt=F32, c=None):
            return (c or ctx).enter_context(nc.sbuf_tensor(name, shape, dt))

        def psum(name, shape, c):
            return c.enter_context(nc.psum_tensor(name, shape, F32))

        def sem(name):
            return ctx.enter_context(nc.semaphore(name))

        hT_hi = sbuf("hT_hi", [P, KC, S], F32R)
        hT_lo = sbuf("hT_lo", [P, KC, S], F32R)
        raw = sbuf("raw", [P, RAW, HALF])
        whi = sbuf("whi", [P, SPLIT, HALF], F32R)
        wlo = sbuf("wlo", [P, SPLIT, HALF], F32R)
        scan_add = sbuf("scan_add", [P, S])
        ident = scan_add[:, 0:P]
        zeros = scan_add[:, P:P + HALF]
        mean_w = sbuf("mean_w", [P, P], F32R)
        gain_pre = sbuf("gain_pre", [P, KC])
        bias_gate = sbuf("bias_gate", [P, 2 * KC])
        gain_head = sbuf("gain_head", [P, 1])
        small = sbuf("small", [P, 64])
        eps_col = small[:, 0:1]
        neg_lam = small[:, 1:2]
        lam_dot = small[:, 2:4]
        lam_exp = small[:, 4:6]
        probe = small[:, 6:7]
        sumsq = small[:, 8:16]
        std = small[:, 16:24]
        rstd = small[:, 24:32]
        stats = small[:, 32:62].rearrange("p (b n) -> p b n", b=ROWS)

        third = [sbuf(f"third{b}", [P, S + 4]) for b in range(2)]
        o_in = [t[:, 0:S] for t in third]

        attn = ExitStack()
        stack = sbuf("stack", [P, 2, 3, S], F32R, attn)
        v_split = sbuf("v_split", [P, NT, 4 * HD], F32R, attn)
        alibi = sbuf("alibi", [P, S], F32, attn)
        pre = ExitStack()
        xt = sbuf("xt", [P, NT, S], F32, pre)
        junk = sbuf("junk", [P, S], F32, pre)
        lam_in = sbuf("lam_in", [P, 2, 2, HD], F32, pre)
        pre.close()
        wT_hi = [sbuf(f"wT_hi{b}", [P, n, 2 * P], F32R, attn) for b, n in enumerate((8, 6))]
        wT_lo = [sbuf(f"wT_lo{b}", [P, n, 2 * P], F32R, attn) for b, n in enumerate((8, 6))]
        stage_hi = sbuf("stage_hi", [P, 2, S], F32R, attn)
        stage_lo = sbuf("stage_lo", [P, 2, S], F32R, attn)
        keep = [sbuf(f"keep{b}", [P, S + 4], F32, attn) for b in range(2)] + [third[1]]
        beta = [sbuf(f"beta{b}", [P, S], F32, attn) for b in range(2)] + [third[0]]
        vT = sbuf("vT", [P, S], F32, attn)
        o_sb = sbuf("o_sb", [P, S], F32, attn)
        attn.close()

        late = ExitStack()
        gated_hi = sbuf("gated_hi", [P, UNITS, S], F32R, late)
        gated_lo = sbuf("gated_lo", [P, UNITS, S], F32R, late)
        zphase = ExitStack()
        early_z = sbuf("early_z", [P, SB_UNITS, S], F32, zphase)
        silu = sbuf("silu", [P, 2, HALF], F32, zphase)
        sq = sbuf("sq", [P, S], F32, zphase)
        sq_hi = sbuf("sq_hi", [P, S], F32R, zphase)
        sq_lo = sbuf("sq_lo", [P, S], F32R, zphase)
        rms = sbuf("rms", [P, S], F32, zphase)
        zphase.close()
        merged = sbuf("merged", [P, KC, S], F32, late)
        last = ExitStack()
        gate = sbuf("gate", [P, 4, HALF], F32, last)
        last.close()
        w_last_most = sbuf("w_last_most", [P, KC - 1, HALF], F32R, late)
        late.close()
        tail = ExitStack()
        x_again = sbuf("x_again", [P, NT, S], F32, tail)
        post = sbuf("post", [P, S], F32, tail)
        junk2 = sbuf("junk2", [P, HALF], F32, tail)
        w_last_lo = sbuf("w_last_lo", [P, KC, HALF], F32R, tail)
        w_last_rest = sbuf("w_last_rest", [P, HALF], F32R, tail)
        w_last_hi = [w_last_most[:, k, :] for k in range(KC - 1)] + [w_last_rest[:]]
        y_right = sbuf("y_right", [P, 2, HALF], F32, tail)
        tail.close()

        pa = ExitStack()
        proj_ps = psum("proj_ps", [P, S], pa)
        score_ps = [psum(f"score_ps{b}", [P, S], pa) for b in range(2)]
        t_ps = psum("t_ps", [P, HALF], pa)
        o_ps = psum("o_ps", [P, HALF], pa)
        pa.close()
        pb = ExitStack()
        bank = psum("bank", [P, 8, HALF], pb)
        pb.close()
        mean_ps = score_ps[0]
        z_ps = [proj_ps, score_ps[1]]

        x_loaded = [sem(f"x_loaded{t}") for t in range(NT)]
        const_loaded = sem("const_loaded")
        lam_loaded = sem("lam_loaded")
        raw_loaded = [sem(f"raw_loaded{b}") for b in range(RAW)]
        consts = sem("consts")
        consts_fixed = sem("consts_fixed")
        w_hi_done = sem("w_hi_done")
        w_ready = sem("w_ready")
        halves_done = sem("halves_done")
        sumsq_done = sem("sumsq_done")
        std_done = sem("std_done")
        rstd_done = sem("rstd_done")
        x_normed = sem("x_normed")
        hT_ps_done = sem("hT_ps_done")
        hT_hi_done = sem("hT_hi_done")
        hT_done = sem("hT_done")
        pads_done = sem("pads_done")
        lam_step = sem("lam_step")
        lam_exp_done = sem("lam_exp_done")
        stage_hi_done = sem("stage_hi_done")
        proj_read = sem("proj_read")
        stack_loaded = [sem(f"stack_loaded{h}") for h in range(2)]
        stack_half = [sem(f"stack_half{n}") for n in range(2)]
        scores_done = sem("scores_done")
        keep_done = sem("keep_done")
        scan_done = sem("scan_done")
        sb_scores_read = sem("sb_scores_read")
        df_scores_read = sem("df_scores_read")
        negmax_done = sem("negmax_done")
        exp_done = sem("exp_done")
        recip_done = sem("recip_done")
        scaled = sem("scaled")
        row_ready = sem("row_ready")
        t_full = sem("t_full")
        t_hi_done = sem("t_hi_done")
        t_free = sem("t_free")
        av_done = sem("av_done")
        table_loaded = sem("table_loaded")
        o_half = sem("o_half")
        o_saved = sem("o_saved")
        o_stored = sem("o_stored")
        z_sig = sem("z_sig")
        z_gated = sem("z_gated")
        z_hi = sem("z_hi")
        z_done = sem("z_done")
        o_loaded = [sem(f"o_loaded{b}") for b in range(2)]
        rms_ln = sem("rms_ln")
        z_silu = sem("z_silu")
        sq_done = sem("sq_done")
        sq_hi_done = sem("sq_hi_done")
        sq_split = sem("sq_split")
        mean_done = sem("mean_done")
        rms_done = sem("rms_done")
        normed = sem("normed")
        gates_done = sem("gates_done")
        y_read = sem("y_read")
        merged_done = sem("merged_done")
        m_hi_done = sem("m_hi_done")
        m_done = sem("m_done")
        out_ps = sem("out_ps")
        sq_half = [sem(f"sq_half{n}") for n in range(2)]
        y_post = sem("y_post")
        y_saved = sem("y_saved")
        y_std = sem("y_std")
        left_mean = sem("left_mean")
        right_done = sem("right_done")
        w_last_hi_done = sem("w_last_hi_done")
        w_last_ready = sem("w_last_ready")
        y_scaled = sem("y_scaled")
        late_loaded = sem("late_loaded")
        xr_loaded = [sem(f"xr_loaded{t}") for t in range(NT)]
        fin_right = sem("fin_right")
        fin_left = sem("fin_left")
        out_stored = sem("out_stored")
        waited = sem("waited")

        f32 = lambda ap: ap.bitcast(F32)

        def x_bank(half, k):
            return k if half == 0 else 2 + k % 6

        def score_shift(i):
            return P + HD if i == 3 else 0

        def score_columns(i):
            bank_end = HALF + score_shift(i)
            if i == NT - 1:
                return [((i - 1) * P, S)]
            return [(i * P, bank_end), (bank_end, S)] if i * P < HALF else [(i * P, S)]

        def score_row(b, i):
            return score_ps[b][:, i * P - score_shift(i):S - score_shift(i)]

        def v_source(un):
            return t_ps[:].rearrange("p (j a c) -> p j a c", j=4, c=HD)

        def v_part(un, n, part):
            blocks = v_split[:, 4 * n:4 * n + 4, :].rearrange("p j (a c) -> p j a c", c=HD)
            return blocks[:, :, part:4:2, :] if un.sb else blocks[:, :, 2 * part:2 * part + 2, :]

        block = ctx.enter_context(nc.Block())

        @block.sync
        def _(sp):
            for t in range(NT):
                sp.dma_start(xt[:, t, :], x[t * P:(t + 1) * P, :]).then_inc(x_loaded[t], 16)
                if t == 3:
                    for s in range(SPLIT):
                        sp.dma_start(raw[:, s, :], w_all[s]).then_inc(raw_loaded[s], 16)
                if t == 0:
                    sp.dma_start(gain_pre[:], norm_pre).then_inc(const_loaded, 16)
                    sp.dma_start(bias_gate[:], b_gate).then_inc(const_loaded, 16)
                    sp.dma_start(gain_head[:], head_norm).then_inc(const_loaded, 16)
            for n, src in enumerate((lam_q, lam_k)):
                sp.dma_start(lam_in[:, n], src.partition_broadcast(P)).then_inc(lam_loaded, 16)
            def load_granule(n, slot):
                sp.wait_ge(w_ready, n + (1 - RAW))
                sp.dma_start(raw[:, slot, :], w_all[n]).then_inc(raw_loaded[slot], 16)

            def load_stack(v, h, cols, done):
                mine = slice(64 * h, 64 * h + 64)
                top, bottom = slice(0, 64), slice(64, 128)
                for n, (dst, src) in enumerate((
                        (stack[top, h, 0:3:2, cols], stage_hi[mine, :, cols]),
                        (stack[bottom, h, 0:3:2, cols], stage_lo[mine, :, cols]),
                        (stack[top, h, 1, cols], stage_lo[mine, 0, cols]),
                        (stack[bottom, h, 1, cols], stage_hi[mine, 0, cols]))):
                    sem_, inc = done[n % len(done)]
                    sp.dma_start(f32(dst), f32(src)).then_inc(sem_, inc)

            def staged(v):
                sp.wait_ge(stage_hi_done, v * 4 + 4)
                sp.wait_ge(proj_read, v * 6 + 4)

            everything = slice(0, S)
            for s in range(SPLIT, RAW):
                sp.dma_start(raw[:, s, :], w_all[s]).then_inc(raw_loaded[s], 16)
            for s in range(RAW):
                load_granule(RAW + s, s)
            staged(0)
            for h in range(2):
                load_stack(0, h, everything, [(stack_loaded[h], 16)])
            with sp.Fori(1, SB_UNITS) as v:
                for s in range(RAW):
                    load_granule(v * G_QKV + (RAW + s), s)
                staged(v)
                for h in range(2):
                    sp.wait_ge(scores_done, v * 16 + (8 * h - 8))
                    load_stack(v, h, everything, [(stack_loaded[h], 16)])
            for v in range(SB_UNITS, UNITS):
                for s in range(RAW):
                    load_granule(v * G_QKV + RAW + s, s)
                staged(v)
                for m in range(2):
                    sp.wait_ge(scores_done, v * 16 + (8 * m - 8))
                    if v == SB_UNITS:
                        load_stack(v, m, everything, [(stack_half[0], 32), (stack_half[1], 32)])
                    else:
                        for h in range(2):
                            load_stack(v, h, slice(m * HALF, (m + 1) * HALF), [(stack_half[m], 16)])
            first = (UNITS + 1) * G_QKV
            with sp.Fori(first // RAW, GRANULES // RAW) as it:
                for s in range(RAW):
                    load_granule(it * RAW + s, s)
            for n in range(GRANULES // RAW * RAW, GRANULES):
                sp.wait_ge(w_last_ready, n - RAW - G_LAST0 + 1)
                sp.dma_start(raw[:, n % RAW, :], w_all[n]).then_inc(raw_loaded[n % RAW], 16)
            sp.wait_ge(halves_done, 2 * G_OUT0)
            sp.dma_start(post[:], norm_post.partition_broadcast(P)).then_inc(late_loaded, 16)
            for t in range(NT):
                sp.dma_start(x_again[:, t, :], x[t * P:(t + 1) * P, :]).then_inc(xr_loaded[t], 16)
            for t in range(NT):
                rows = slice(t * P, (t + 1) * P)
                sp.wait_ge(fin_right, t + 1)
                sp.dma_start(out[rows, HALF:], x_again[:, t, HALF:]).then_inc(out_stored, 16)
                sp.wait_ge(fin_left, t + 1)
                sp.dma_start(out[rows, 0:HALF], x_again[:, t, 0:HALF]).then_inc(out_stored, 16)
            sp.wait_ge(out_stored, 32 * NT)

        @block.gpsimd
        def _(pool):
            pool.memset(scan_add[:], 0.0).then_inc(consts, 1)
            pool.wait_ge(consts, 1)
            pool.affine_select(out=ident, in_=ident, compare_op=ALU.not_equal, fill=1.0, base=0,
                               pattern=[[-1, P]], channel_multiplier=1).then_inc(consts, 1)
            pool.iota(alibi[:], pattern=[[-1, S]], base=0, channel_multiplier=1,
                      allow_small_or_imprecise_dtypes=True).then_inc(consts, 1)

            def split(g, s, wait_used):
                pool.wait_ge(raw_loaded[s], g_loads(g, s))
                if wait_used:
                    early = 1 if isinstance(g, int) and g == SPLIT else 0
                    pool.wait_ge(halves_done, g * 2 + (2 * (1 - SPLIT) + early))
                pool.tensor_tensor(whi[:, s % SPLIT, :], raw[:, s, :], zeros, ALU.add).then_inc(w_hi_done, 1)
                pool.wait_ge(w_hi_done, g + 1)
                pool.tensor_tensor(wlo[:, s % SPLIT, :], raw[:, s, :], f32(whi[:, s % SPLIT, :]),
                                   ALU.subtract).then_inc(w_ready, 1)

            loads = [16]

            def g_loads(g, s):
                return loads[0]

            for s in range(RAW):
                split(s, s, s >= SPLIT)
            with pool.Fori(1, G_LAST0 // RAW) as it:
                loads[0] = it * 16 + 16
                for s in range(RAW):
                    split(it * RAW + s, s, True)

        @block.tensor
        def _(pe):
            def three(ps, a_hi, a_lo, b_hi, b_lo, first, last):
                pe.matmul(ps, a_hi, b_hi, start=first, stop=False)
                pe.matmul(ps, a_hi, b_lo, start=False, stop=False)
                return pe.matmul(ps, a_lo, b_hi, start=False, stop=last)

            def transpose_x(half, k):
                for t in range(4):
                    mm = pe.transpose(bank[:, x_bank(half, k), t * P:(t + 1) * P],
                                      xt[:, 4 * half + t, k * P:(k + 1) * P], ident)
                mm.then_inc(hT_ps_done, 1)

            pe.wait_ge(consts, 2)
            pe.wait_ge(x_normed, 4)
            for k in range(KC):
                transpose_x(0, k)
            pe.sem_inc(av_done, 2)

            def w_tile(a, kk):
                return (whi[:, a, kk * P:(kk + 1) * P], wlo[:, a, kk * P:(kk + 1) * P])

            def project(g0, half0, c, skip_wait=False, ps2=proj_ps):
                _, a, n, pair = chunk_parts(c)
                if pair == 0:
                    if n == 0:
                        pe.wait_ge(w_ready, g0 + (a + 1))
                    if a == 0 and not skip_wait:
                        pe.wait_ge(proj_read, half0 + (n - 1))
                ps = ps2[:, n * HALF:(n + 1) * HALF]
                for kk in (2 * pair, 2 * pair + 1):
                    k = 4 * a + kk
                    hi, lo = w_tile(a, kk)
                    mm = three(ps, hi, lo, hT_hi[:, k, n * HALF:(n + 1) * HALF],
                               hT_lo[:, k, n * HALF:(n + 1) * HALF], k == 0, k == KC - 1)
                if pair == 1:
                    mm.then_inc(halves_done, 1)

            def project_chunk(v, c):
                b = c // 8
                if v is None:
                    project(G_Z0 + 2 * b, 6 * UNITS + 2 * b, c % 8)
                else:
                    project(v * G_QKV + 2 * b, v * 6 + 2 * b, c % 8,
                            skip_wait=isinstance(v, int) and v == 0 and b == 0)

            def transpose_v(un, n):
                pe.wait_ge(t_free, un.t(n + 1))
                if n == 0:
                    pe.wait_ge(proj_read, un.per(6, 6))
                for b in range(4):
                    j = 4 * n + b
                    mm = pe.transpose(t_ps[:, b * P:(b + 1) * P], vT[:, j * P:(j + 1) * P], ident)
                mm.then_inc(t_full, 1)

            def scores(un, n):
                h, i = (n // NT, n % NT) if un.sb else (n % 2, n // 2)
                free = sb_scores_read if un.sb else df_scores_read
                pe.wait_ge(free, un.i * 16 + (n + 1))
                if i == 0 and un.sb:
                    pe.wait_ge(stack_loaded[h], un.i * 64 + 64)
                if i == 0 and not un.sb:
                    for part in range(2):
                        pe.wait_ge(stack_half[part], un.i * 128 + 128)
                ps, shift = score_ps[n % 2], score_shift(i)
                for c0, c1 in score_columns(i):
                    o = ps[:, c0 - shift:c1 - shift]
                    kk = stack[:, h, 2, c0:c1]
                    q1 = stack[:, h, 0, i * P:(i + 1) * P]
                    q2 = stack[:, h, 1, i * P:(i + 1) * P]
                    pe.matmul(o, q1, kk, start=True, stop=False)
                    mm = pe.matmul(o, q2, kk, start=False, stop=True)
                mm.then_inc(scores_done, 1)

            def transpose_row(un, n, k):
                h, i = un.kind.slots[n]
                pe.wait_ge(t_free, un.t(un.kind.first_use[n] + k + 1))
                if k == 0:
                    pe.wait_ge(row_ready, un.w(n + 1))
                for b, j in enumerate(un.kind.uses[n][k]):
                    mm = pe.transpose(t_ps[:, b * P:(b + 1) * P], beta[n % ROWS][:, (j - i) * P:(j - i + 1) * P],
                                      ident)
                mm.then_inc(t_full, 1)

            def attend(un, grp):
                h, i0 = un.kind.slots[2 * grp]
                pe.wait_ge(t_free, un.t(un.kind.first_use[2 * grp + 1] + len(un.kind.uses[2 * grp + 1]) + 1))
                pe.wait_ge(o_saved, un.g(grp + 1))
                o = o_ps[:, 0:2 * P]
                for jr in range(NT - i0):
                    j = i0 + jr
                    w_hi, w_lo = wT_hi[grp % 2][:, jr, :], wT_lo[grp % 2][:, jr, :]
                    if un.sb:
                        v = v_split[:, j, 2 * HD * h:2 * HD * (h + 1)]
                        pe.matmul(o, v, w_hi, start=jr == 0, stop=False)
                        mm = pe.matmul(o, v, w_lo, start=False, stop=j == NT - 1)
                    else:
                        mm = three(o, v_split[:, j, 0:P], v_split[:, j, P:2 * P], w_hi, w_lo, jr == 0, j == NT - 1)
                mm.then_inc(av_done, 1)

            def unit(un, nxt):
                ns = len(un.kind.slots)
                plan = plan_of(un, nxt)
                chunks = numbered(plan["chunks"])

                def project_chunks(some):
                    for c in some:
                        project_chunk(nxt, c)

                def slot_scores(n):
                    if n < ns and un.sb:
                        scores(un, n)
                    elif n < ns:
                        for c in range(2):
                            scores(un, 2 * n + c)

                transpose_v(un, 0)
                slot_scores(0)
                if un.sb:
                    slot_scores(1)
                project_chunks(chunks[0][0])
                transpose_v(un, 1)
                project_chunks(chunks[0][1])
                if not un.sb:
                    slot_scores(1)
                project_chunks(chunks[0][2])
                for n in range(ns):
                    late = chunks[n + 1]
                    ahead = [r + 1 for r in rows_of(plan, n)]
                    for step in plan["pe"]:
                        if step == "transposes":
                            transpose_row(un, n, 0)
                        elif step == "more transposes":
                            for k in range(1, len(un.kind.uses[n])):
                                transpose_row(un, n, k)
                        elif step == "attend" and n >= 2 and n % 2 == 0:
                            attend(un, n // 2 - 1)
                        elif step == "scores":
                            slot_scores(ahead[0])
                        elif step.startswith("chunks"):
                            project_chunks(late[int(step[-1])])
                    for r in ahead[1:]:
                        slot_scores(r)
                attend(un, ns // 2 - 1)

            first = (0, 1, 4, 5, 2, 3, 6, 7)
            for at, c in enumerate(first):
                if at == 3:
                    pe.wait_ge(x_normed, NT)
                    for k in range(KC):
                        pe.wait_ge(hT_done, k + 3 if k < 6 else KC + k - 5)
                        transpose_x(1, k)
                pe.wait_ge(hT_done, 2 * at + 2)
                project_chunk(0, c)
            for c in range(8, 24):
                project_chunk(0, c)
            pe.wait_ge(pads_done, ROWS)
            with pe.Fori(0, SB_UNITS) as i:
                unit(Unit(SB, i), i + 1)
            with pe.Fori(0, DF_UNITS - 1) as i:
                unit(Unit(DF, i), i + (SB_UNITS + 1))
            unit(Unit(DF, DF_UNITS - 1), None)

            def mean_square(j):
                for n in range(2):
                    pe.wait_ge(sq_split, j * 2 + (n + 1))
                    o = mean_ps[:, n * HALF:(n + 1) * HALF]
                    cols = slice(n * HALF, (n + 1) * HALF)
                    pe.matmul(o, mean_w[:], sq_hi[:, cols], start=True, stop=False)
                    pe.matmul(o, mean_w[:], sq_lo[:, cols], start=False, stop=True).then_inc(mean_done, 1)

            for c in range(sum(map(sum, LAST_PLAN["chunks"])), 8 * SB_UNITS):
                project_chunk(None, c)
            for j in range(DF_UNITS):
                g0, half0 = 2 * j + G_Z0 + 2 * SB_UNITS, 2 * j + 6 * UNITS + 2 * SB_UNITS
                if j == 1:
                    pe.wait_ge(df_scores_read, 16 * DF_UNITS + 2)
                for c in range(8):
                    if c == 4:
                        mean_square(j)
                    project(g0, half0 if j == 0 else half0 - 2, c, skip_wait=j == 1, ps2=z_ps[j % 2])

            with pe.Fori(0, KC) as m:
                for b in range(2):
                    for a in range(2):
                        pe.wait_ge(w_ready, m * 6 + (G_FIN0 + 2 * b + a + 1))
                        for n in range(2):
                            if a == 0:
                                pe.wait_ge(gates_done, m * 4 + (2 * b + n + 1))
                            for kk in range(4):
                                k = 4 * a + kk
                                hi, lo = w_tile(a, kk)
                                mm = three(bank[:, 2 * b + n, :], hi, lo, hT_hi[:, k, n * HALF:(n + 1) * HALF],
                                           hT_lo[:, k, n * HALF:(n + 1) * HALF], k == 0, k == KC - 1)
                            mm.then_inc(halves_done, 1)
                for b in range(2):
                    pe.wait_ge(w_ready, m * 6 + (G_FIN0 + 4 + b + 1))
                    for n in range(2):
                        pe.wait_ge(y_read, m * 4 + (2 * b + n + 1))
                        for kk in range(4):
                            if b == 0 and n == 0:
                                pe.wait_ge(z_done, 2 * (DF_UNITS + kk + 1) + 2)
                            hi, lo = w_tile(b, kk)
                            mm = three(bank[:, 4 + 2 * b + n, :], hi, lo,
                                       gated_hi[:, 4 * b + kk, n * HALF:(n + 1) * HALF],
                                       gated_lo[:, 4 * b + kk, n * HALF:(n + 1) * HALF], kk == 0, kk == 3)
                        mm.then_inc(halves_done, 1)

            def output_product(t, k, w_hi, w_lo):
                return three(bank[:, t, :], hT_hi[:, k, t * P:(t + 1) * P], hT_lo[:, k, t * P:(t + 1) * P],
                             w_hi, w_lo, k == 0, k == KC - 1)

            for k in range(KC):
                g = G_OUT0 + k
                pe.wait_ge(w_ready, g + 1)
                pe.wait_ge(m_done, k + 1)
                for t in range(NT):
                    if k == 0:
                        pe.wait_ge(*((gates_done, 4 * KC + 4) if t < 4 else (y_read, 4 * KC + 4)))
                    mm = output_product(t, k, whi[:, g % SPLIT, :], wlo[:, g % SPLIT, :])
                    if k == KC - 1 and t < NT - 1:
                        mm.then_inc(out_ps, 1)
                    elif t == NT - 1:
                        mm.then_inc(halves_done, 2)
            for t in range(NT):
                pe.wait_ge(y_saved, t + 1)
                for k in range(KC):
                    if t == 0:
                        pe.wait_ge(w_last_ready, k + 1)
                    mm = output_product(t, k, w_last_hi[k], w_last_lo[:, k, :])
                mm.then_inc(right_done, 1)

        @block.scalar
        def _(act):
            def copy(dst, src, scale=1.0):
                return act.activation(dst, src, ACT.Copy, scale=scale)

            act.sem_inc(sb_scores_read, 2)
            act.sem_inc(o_saved, 1)
            act.sem_inc(o_stored, 16)

            act.wait_ge(consts_fixed, 1)
            act.activation(std[:, 0:1], eps_col, ACT.Sqrt).then_inc(std_done, 1)
            act.wait_ge(std_done, 1)
            def sumsq_row_tile(t):
                act.wait_ge(x_loaded[t], 16)
                act.activation(junk[:], xt[:, t, :], ACT.Square,
                               accum_out=sumsq[:, t:t + 1]).then_inc(sumsq_done, 1)
                act.wait_ge(sumsq_done, t + 1)
                act.activation(std[:, t:t + 1], sumsq[:, t:t + 1], ACT.Sqrt, bias=eps_col,
                               scale=1.0 / D).then_inc(std_done, 1)

            def hT_hi_part(q):
                half, k = q // KC, q % KC
                act.wait_ge(hT_ps_done, q + 1)
                act.activation(hT_hi[:, k, half * HALF:(half + 1) * HALF], bank[:, x_bank(half, k), :], ACT.Copy,
                               scale=gain_pre[:, k:k + 1]).then_inc(hT_hi_done, 1)

            act.wait_ge(const_loaded, 48)
            for t in range(NT):
                sumsq_row_tile(t)
                if t >= 4:
                    for q in range(2 * (t - 4), 2 * (t - 4) + 2):
                        hT_hi_part(q)
            for q in range(KC, 2 * KC):
                hT_hi_part(q)
            act.wait_ge(lam_step, 2)
            act.activation(lam_exp, lam_dot, ACT.Exp).then_inc(lam_exp_done, 1)

            def stage(v, c):
                b, _, n, _ = chunk_parts(c)
                if v is None or b == 2 or not completes(c):
                    return
                act.wait_ge(halves_done, v * (2 * G_QKV) + (2 * (2 * b + 1) + n + 1))
                if b == 0 and n == 0:
                    stage_is_free(v)
                copy(stage_hi[:, b, n * HALF:(n + 1) * HALF], proj_ps[:, n * HALF:(n + 1) * HALF],
                     HD ** -0.5 if b == 0 else 1.0).then_inc(stage_hi_done, 1)

            def stage_is_free(v):
                if isinstance(v, int) and v == 0:
                    return
                if loop_kind[0] is SB:
                    for h in range(2):
                        act.wait_ge(stack_loaded[h], v * 64)
                else:
                    for part in range(2):
                        act.wait_ge(stack_half[part], v * 128 - 128 * SB_UNITS)

            loop_kind = [SB]

            def t_hi(un, n, k):
                kind = un.kind
                h, i = kind.slots[n]
                grp = n // 2
                i0 = kind.slots[2 * grp][1]
                blocks = kind.uses[n][k]
                act.wait_ge(t_full, un.t(kind.first_use[n] + k + 1))
                if n % 2 == 0 and k == 0:
                    act.wait_ge(av_done, un.g(grp + 1))
                j0 = blocks[0] - i0
                copy(wT_hi[grp % 2][:, j0:j0 + len(blocks), (n % 2) * P:(n % 2 + 1) * P],
                     t_ps[:, 0:len(blocks) * P].rearrange("p (j c) -> p j c", c=P)).then_inc(t_hi_done, 1)

            def v_hi_part(un, n):
                act.wait_ge(t_full, un.t(n + 1))
                if n == 0:
                    act.wait_ge(av_done, un.g(2))
                copy(v_part(un, n, 0), v_source(un)).then_inc(t_hi_done, 1)

            def save_o(un, grp):
                h, i0 = un.kind.slots[2 * grp]
                act.wait_ge(av_done, un.g(grp + 3))
                if grp == 0:
                    act.wait_ge(o_stored, un.per(16, 16))
                cols = slice(i0 * P, (i0 + 2) * P)
                if un.sb:
                    mine, other = slice(64 * h, 64 * h + 64), slice(64 - 64 * h, 128 - 64 * h)
                    copy(o_sb[mine, cols], o_ps[other, 0:2 * P]).then_inc(o_half, 1)
                else:
                    copy(o_sb[:, cols], o_ps[:, 0:2 * P]).then_inc(o_saved, 1)

            def sb_sigmoid(un, n, which):
                h, i = un.kind.slots[n]
                width = S - i * P
                if which == 0:
                    act.wait_ge(scores_done, un.per(16, n + 1))
                    act.wait_ge(t_full, un.row_free(n))
                    act.activation(keep[n % ROWS][:, 1:1 + width], score_row(n % 2, i), ACT.Sigmoid,
                                   scale=-1.0).then_inc(keep_done, 1)
                else:
                    act.activation(beta[n % ROWS][:, 0:width], score_row(n % 2, i),
                                   ACT.Sigmoid).then_inc(sb_scores_read, 1)

            def df_exp(un, n, c):
                h, i = un.kind.slots[n]
                width = S - i * P
                row = (beta, keep)[c][n % ROWS][:, 0:width]
                act.wait_ge(negmax_done, un.i * 16 + (2 * n + c + 1))
                act.activation(row, row, ACT.Exp, bias=stats[:, n % ROWS, 2 + c:3 + c],
                               accum_out=stats[:, n % ROWS, 4 + c:5 + c]).then_inc(exp_done, 1)

            def unit(un, nxt):
                ns = len(un.kind.slots)
                plan = plan_of(un, nxt)
                chunks = numbered(plan["chunks"])
                loop_kind[0] = un.kind

                def first_part(n):
                    if n < ns and un.sb:
                        sb_sigmoid(un, n, 0)
                    elif n < ns:
                        df_exp(un, n, 0)

                def second_part(n):
                    if n < ns and un.sb:
                        sb_sigmoid(un, n, 1)
                    elif n < ns:
                        df_exp(un, n, 1)

                act.activation(probe, eps_col, ACT.Sigmoid if un.sb else ACT.Exp).then_inc(table_loaded, 1)
                act.wait_ge(table_loaded, un.u + 1)
                v_hi_part(un, 0)
                if un.sb:
                    first_part(0)
                    second_part(0)
                v_hi_part(un, 1)
                if not un.sb:
                    first_part(0)
                    second_part(0)
                for n in range(ns):
                    ahead = rows_of(plan, n)
                    for step in plan["act"]:
                        if step == "hi":
                            t_hi(un, n, 0)
                        elif step == "more hi":
                            for k in range(1, len(un.kind.uses[n])):
                                t_hi(un, n, k)
                        elif step == "row a":
                            first_part(ahead[0])
                        elif step == "row b":
                            second_part(ahead[0])
                        elif step == "output" and n >= 2 and n % 2 == 0:
                            save_o(un, n // 2 - 1)
                        elif step == "stage":
                            for c in sum(chunks[n], []):
                                stage(nxt, c)
                    for r in ahead[1:]:
                        first_part(r)
                        second_part(r)
                    if nxt is None and n == ns - 2:
                        for p in range(2):
                            load_o(p)
                for c in sum(chunks[ns], []):
                    stage(nxt, c)
                if nxt is None:
                    squares(0)
                save_o(un, ns // 2 - 1)
                act.wait_ge(o_saved, un.g(ns // 2 + 1))
                act.dma_start(o_dram[un.u], o_sb[:]).then_inc(o_stored, 16)

            for c in range(24):
                stage(0, c)
            with act.Fori(0, SB_UNITS) as i:
                unit(Unit(SB, i), i + 1)
            with act.Fori(0, DF_UNITS - 1) as i:
                unit(Unit(DF, i), i + (SB_UNITS + 1))

            def load_o(p):
                if Z_ORDER[p] == UNITS - 1:
                    act.wait_ge(o_stored, 16 * UNITS + 16)
                act.dma_start(o_in[p % 2], o_dram[Z_ORDER[p]]).then_inc(o_loaded[p % 2], 16)

            def z_sigmoid(p, n, src):
                act.wait_ge(z_done, p * 2 + (n + 1))
                act.activation(silu[:, n, :], src, ACT.Sigmoid).then_inc(z_sig, 1)

            def z_hi_part(p, n):
                act.wait_ge(z_gated, p * 2 + (n + 1))
                copy(gated_hi[:, Z_ORDER[p], n * HALF:(n + 1) * HALF], silu[:, n, :]).then_inc(z_hi, 1)

            def squares(j):
                act.wait_ge(o_loaded[j % 2], 16 * (j // 2 + 1))
                for n in range(2):
                    cols = slice(n * HALF, (n + 1) * HALF)
                    act.activation(sq[:, cols], o_in[j % 2][:, cols], ACT.Square).then_inc(sq_done, 1)
                for n in range(2):
                    cols = slice(n * HALF, (n + 1) * HALF)
                    act.wait_ge(sq_done, j * 2 + (n + 1))
                    copy(sq_hi[:, cols], sq[:, cols]).then_inc(sq_hi_done, 1)

            def inverse_rms(j):
                for n in range(2):
                    act.wait_ge(mean_done, j * 2 + (n + 1))
                    act.activation(rms[:, n * HALF:(n + 1) * HALF], mean_ps[:, n * HALF:(n + 1) * HALF],
                                   ACT.Ln, bias=eps_col).then_inc(rms_ln, 1)
                for n in range(2):
                    act.wait_ge(rms_ln, j * 2 + (n + 1))
                    half = rms[:, n * HALF:(n + 1) * HALF]
                    act.activation(half, half, ACT.Exp, scale=-0.5).then_inc(rms_done, 1)

            unit(Unit(DF, DF_UNITS - 1), None)
            for p, v in enumerate(Z_ORDER):
                if v >= SB_UNITS:
                    inverse_rms(p)
                    if p == DF_UNITS - 1:
                        act.sem_inc(gates_done, 2)
                    else:
                        squares(p + 1)
                else:
                    act.wait_ge(proj_read, 6 * UNITS + 2 * SB_UNITS)
                for n in range(2):
                    cols = slice(n * HALF, (n + 1) * HALF)
                    if v >= SB_UNITS:
                        act.wait_ge(halves_done, v * 4 + (2 * G_Z0 + 2 + n + 1))
                        z_sigmoid(p, n, z_ps[p % 2][:, cols])
                    else:
                        z_sigmoid(p, n, early_z[:, v, cols])
                for n in range(2):
                    z_hi_part(p, n)
                if p + 2 < UNITS:
                    load_o(p + 2)
                if p == DF_UNITS - 2:
                    act.sem_inc(gates_done, 2)

            with act.Fori(0, KC) as m:
                for b in range(2):
                    for n in range(2):
                        q = 2 * b + n
                        act.wait_ge(halves_done, m * 12 + (2 * (G_FIN0 + 2 * b + 1) + n + 1))
                        act.wait_ge(merged_done, m * 2 + 2)
                        act.sem_inc(waited, 1)
                        act.activation(gate[:, q, :], bank[:, q, :], ACT.Sigmoid,
                                       bias=bias_gate[:, bass.ds(m + b * KC, 1)]).then_inc(gates_done, 1)

            for k in range(KC):
                act.wait_ge(merged_done, 2 * (k + 1) + 2)
                copy(hT_hi[:, k, :], merged[:, k, :]).then_inc(m_hi_done, 1)
            act.wait_ge(halves_done, 2 * G_OUT0)
            act.wait_ge(m_done, KC)
            for k in range(KC):
                g = G_LAST0 + k
                act.wait_ge(raw_loaded[g % RAW], 16 * (g // RAW) + 16)
                copy(w_last_hi[k], raw[:, g % RAW, :]).then_inc(w_last_hi_done, 1)
            act.activation(std[:, 0:1], eps_col, ACT.Sqrt).then_inc(y_std, 1)
            act.wait_ge(y_std, 1)
            for t in range(NT):
                act.wait_ge(y_saved, t + 1)
                if t:
                    act.wait_ge(sq_half[0], t)
                act.activation(junk2[:], merged[:, t, 0:HALF], ACT.Square,
                               accum_out=sumsq[:, t:t + 1]).then_inc(sq_half[0], 1)
            act.wait_ge(sq_half[0], NT)
            for t in range(NT):
                act.wait_ge(right_done, t + 1)
                act.activation(junk2[:], bank[:, t, :], ACT.Square,
                               accum_out=std[:, t:t + 1]).then_inc(sq_half[1], 1)
                act.wait_ge(sq_half[1], t + 1)
                act.wait_ge(left_mean, 1)
                act.activation(std[:, t:t + 1], std[:, t:t + 1], ACT.Sqrt, bias=sumsq[:, t:t + 1],
                               scale=1.0 / D).then_inc(y_std, 1)

        @block.vector
        def _(dve):
            dve.memset(eps_col, EPS).then_inc(consts_fixed, 1)
            dve.wait_ge(consts, 3)
            dve.scalar_tensor_tensor(alibi[:], alibi[:], -1.0, alibi[:], ALU.mult, ALU.min).then_inc(consts_fixed, 1)
            dve.wait_ge(consts_fixed, 2)
            dve.tensor_scalar(alibi[:], alibi[:], 0.25, None, ALU.mult).then_inc(consts_fixed, 1)
            dve.wait_ge(consts_fixed, 3)
            dve.memset(alibi[64:128, 0:64], -3e38).then_inc(consts_fixed, 1)
            dve.wait_ge(consts_fixed, 4)
            dve.sem_inc(t_free, 1)

            def norm_row_tile(t):
                dve.wait_ge(std_done, t + 2)
                dve.reciprocal(rstd[:, t:t + 1], std[:, t:t + 1]).then_inc(rstd_done, 1)
                dve.wait_ge(rstd_done, t + 1)
                dve.tensor_scalar(xt[:, t, :], xt[:, t, :], rstd[:, t:t + 1], None, ALU.mult)\
                   .then_inc(x_normed, 1)

            def hT_lo_part(q):
                half, k = q // KC, q % KC
                cols = slice(half * HALF, (half + 1) * HALF)
                dve.wait_ge(hT_hi_done, q + 1)
                dve.scalar_tensor_tensor(hT_lo[:, k, cols], bank[:, x_bank(half, k), :], gain_pre[:, k:k + 1],
                                         f32(hT_hi[:, k, cols]), ALU.mult, ALU.subtract).then_inc(hT_done, 1)

            dve.wait_ge(const_loaded, 48)
            for t in range(NT):
                norm_row_tile(t)
                if t >= 4:
                    for q in range(2 * (t - 4), 2 * (t - 4) + 2):
                        hT_lo_part(q)
            dve.wait_ge(lam_loaded, 32)
            dve.tensor_tensor(lam_in[:, 0], lam_in[:, 0], lam_in[:, 1], ALU.mult).then_inc(lam_step, 1)
            dve.wait_ge(lam_step, 1)
            dve.tensor_reduce(lam_dot, lam_in[:, 0], AX.X, ALU.add).then_inc(lam_step, 1)
            for q in range(KC, 2 * KC):
                hT_lo_part(q)
            dve.wait_ge(lam_exp_done, 1)
            dve.tensor_tensor(neg_lam, lam_exp[:, 1:2], lam_exp[:, 0:1], ALU.subtract).then_inc(lam_step, 1)
            dve.wait_ge(lam_step, 3)
            dve.tensor_scalar(neg_lam, neg_lam, -LAMBDA_INIT, None, ALU.add).then_inc(lam_step, 1)
            dve.tensor_scalar(gain_head[:], gain_head[:], 1.0 - LAMBDA_INIT, None, ALU.mult).then_inc(lam_step, 1)
            dve.memset(f32(mean_w[:]), 1.0 / P)
            for b in range(2):
                dve.memset(f32(wT_hi[b][:, 0, P:2 * P]), 0.0)
                dve.memset(f32(wT_lo[b][:, 0, P:2 * P]), 0.0)
            for b in range(ROWS):
                dve.memset(keep[b][:, 0:1], 0.0).then_inc(pads_done, 1)

            def stage(v, c):
                b, _, n, _ = chunk_parts(c)
                if not completes(c):
                    return
                cols = slice(n * HALF, (n + 1) * HALF)
                ps = proj_ps[:, cols]
                if v is None:
                    dve.wait_ge(halves_done, 2 * (G_Z0 + 2 * b + 1) + n + 1)
                    if b == 0 and n == 0:
                        for part in range(2):
                            dve.wait_ge(stack_half[part], 128 * DF_UNITS)
                    dve.tensor_copy(early_z[:, b, cols], ps).then_inc(proj_read, 1)
                elif b == 2:
                    dve.wait_ge(halves_done, v * (2 * G_QKV) + (2 * (2 * b + 1) + n + 1))
                    dve.tensor_copy(vT[:, cols], ps).then_inc(proj_read, 1)
                else:
                    dve.wait_ge(stage_hi_done, v * 4 + (2 * b + n + 1))
                    if b == 0:
                        dve.scalar_tensor_tensor(stage_lo[:, b, cols], ps, HD ** -0.5, f32(stage_hi[:, b, cols]),
                                                 ALU.mult, ALU.subtract).then_inc(proj_read, 1)
                    else:
                        dve.tensor_tensor(stage_lo[:, b, cols], ps, f32(stage_hi[:, b, cols]),
                                          ALU.subtract).then_inc(proj_read, 1)

            def t_lo(un, n, k):
                kind = un.kind
                grp = n // 2
                i0 = kind.slots[2 * grp][1]
                blocks = kind.uses[n][k]
                dve.wait_ge(t_hi_done, un.t(kind.first_use[n] + k + 1))
                j0 = blocks[0] - i0
                cols = slice((n % 2) * P, (n % 2 + 1) * P)
                dve.tensor_tensor(wT_lo[grp % 2][:, j0:j0 + len(blocks), cols],
                                  t_ps[:, 0:len(blocks) * P].rearrange("p (j c) -> p j c", c=P),
                                  f32(wT_hi[grp % 2][:, j0:j0 + len(blocks), cols]),
                                  ALU.subtract).then_inc(t_free, 1)

            def v_lo_part(un, n):
                dve.wait_ge(t_hi_done, un.t(n + 1))
                dve.tensor_tensor(v_part(un, n, 1), v_source(un), f32(v_part(un, n, 0)),
                                  ALU.subtract).then_inc(t_free, 1)

            def add_o(un, grp):
                if un.sb:
                    h, i0 = un.kind.slots[2 * grp]
                    rows, cols = slice(64 * h, 64 * h + 64), slice(i0 * P, (i0 + 2) * P)
                    dve.wait_ge(o_half, un.i * un.kind.per_g + (grp + 1))
                    dve.tensor_tensor(o_sb[rows, cols], o_ps[rows, 0:2 * P], o_sb[rows, cols],
                                      ALU.add).then_inc(o_saved, 1)

            def sb_scan(un, n):
                i = un.kind.slots[n][1]
                width = S - i * P
                k = keep[n % ROWS][:, 1:1 + width]
                dve.wait_ge(keep_done, un.per(16, n + 1))
                dve.tensor_tensor_scan(k, k, scan_add[:, 0:width], 0.0,
                                       ALU.mult, ALU.add).then_inc(scan_done, 1)

            def sb_weights(un, n):
                i = un.kind.slots[n][1]
                width = S - i * P
                dve.wait_ge(sb_scores_read, un.per(16, n + 3))
                dve.wait_ge(scan_done, un.per(16, n + 1))
                dve.tensor_tensor(beta[n % ROWS][:, 0:width], beta[n % ROWS][:, 0:width], keep[n % ROWS][:, 0:width],
                                  ALU.mult).then_inc(row_ready, 1)

            def df_logits(un, n, c):
                i = un.kind.slots[n][1]
                width = S - i * P
                st = stats[:, n % ROWS]
                if c == 0:
                    dve.wait_ge(t_full, un.row_free(n))
                dve.wait_ge(scores_done, un.per(16, 2 * n + c + 1))
                dve.sem_inc(waited, 1)
                dve.tensor_tensor_reduce(out=(beta, keep)[c][n % ROWS][:, 0:width], in0=score_row(c, i),
                                         in1=alibi[:, 0:width], scale=1.0, scalar=-3.4e38, op0=ALU.add,
                                         op1=ALU.max, accum_out=st[:, c:c + 1]).then_inc(df_scores_read, 1)
                dve.wait_ge(df_scores_read, un.i * 16 + (2 * n + c + 3))
                dve.tensor_scalar(st[:, 2 + c:3 + c], st[:, c:c + 1], -1.0, None, ALU.mult).then_inc(negmax_done, 1)

            def df_weights(un, n):
                i = un.kind.slots[n][1]
                width = S - i * P
                st = stats[:, n % ROWS]
                p1, p2 = beta[n % ROWS][:, 0:width], keep[n % ROWS][:, 0:width]
                dve.wait_ge(exp_done, un.i * 16 + (2 * n + 2))
                dve.reciprocal(st[:, 6:8], st[:, 4:6]).then_inc(recip_done, 1)
                dve.wait_ge(recip_done, un.i * NT + (n + 1))
                dve.tensor_scalar(st[:, 8:9], st[:, 7:8], neg_lam, None, ALU.mult).then_inc(scaled, 1)
                dve.tensor_scalar(p1, p1, st[:, 6:7], None, ALU.mult).then_inc(scaled, 1)
                dve.wait_ge(scaled, un.i * 16 + (2 * n + 2))
                dve.scalar_tensor_tensor(p1, p2, st[:, 8:9], p1, ALU.mult, ALU.add).then_inc(row_ready, 1)

            def unit(un, nxt):
                ns = len(un.kind.slots)
                plan = plan_of(un, nxt)
                chunks = numbered(plan["chunks"])

                def first_part(n):
                    if n < ns and un.sb:
                        sb_scan(un, n)
                    elif n < ns:
                        df_logits(un, n, 0)

                def second_part(n):
                    if n < ns and un.sb:
                        sb_weights(un, n)
                    elif n < ns:
                        df_logits(un, n, 1)

                v_lo_part(un, 0)
                first_part(0)
                if un.sb:
                    second_part(0)
                v_lo_part(un, 1)
                if not un.sb:
                    second_part(0)
                    df_weights(un, 0)
                for n in range(ns):
                    ahead = rows_of(plan, n)
                    for step in plan["dve"]:
                        if step == "lo":
                            t_lo(un, n, 0)
                        elif step == "more lo":
                            for k in range(1, len(un.kind.uses[n])):
                                t_lo(un, n, k)
                        elif step == "row a":
                            first_part(ahead[0])
                        elif step == "row b":
                            second_part(ahead[0])
                        elif step == "output" and n >= 2 and n % 2 == 0:
                            add_o(un, n // 2 - 1)
                        elif step == "weights" and ahead[0] < ns and not un.sb:
                            df_weights(un, ahead[0])
                        elif step == "stage":
                            for c in sum(chunks[n], []):
                                stage(nxt, c)
                    for r in ahead[1:]:
                        first_part(r)
                        second_part(r)
                        if not un.sb:
                            df_weights(un, r)
                for c in sum(chunks[ns], []):
                    stage(nxt, c)
                if nxt is None:
                    sq_lo_part(0)
                add_o(un, ns // 2 - 1)

            for c in range(24):
                stage(0, c)
            with dve.Fori(0, SB_UNITS) as i:
                unit(Unit(SB, i), i + 1)
            dve.sem_inc(df_scores_read, 2)
            with dve.Fori(0, DF_UNITS - 1) as i:
                unit(Unit(DF, i), i + (SB_UNITS + 1))
                dve.tensor_scalar(alibi[:], alibi[:], 0.25, None, ALU.mult).then_inc(consts_fixed, 1)
                dve.wait_ge(consts_fixed, i + 5)
            def z_half(p, n, z, step, ready):
                dve.wait_ge(z_sig, p * 2 + (n + 1))
                dve.tensor_tensor(silu[:, n, :], z, silu[:, n, :], ALU.mult).then_inc(step, 1)
                dve.wait_ge(step, ready)
                dve.tensor_tensor(silu[:, n, :], silu[:, n, :], o_in[p % 2][:, n * HALF:(n + 1) * HALF],
                                  ALU.mult).then_inc(z_gated, 1)

            def z_lo_part(p, n):
                cols = slice(n * HALF, (n + 1) * HALF)
                dve.wait_ge(z_hi, p * 2 + (n + 1))
                dve.tensor_tensor(gated_lo[:, Z_ORDER[p], cols], silu[:, n, :],
                                  f32(gated_hi[:, Z_ORDER[p], cols]), ALU.subtract).then_inc(z_done, 1)

            def sq_lo_part(j):
                for n in range(2):
                    cols = slice(n * HALF, (n + 1) * HALF)
                    dve.wait_ge(sq_hi_done, j * 2 + (n + 1))
                    dve.tensor_tensor(sq_lo[:, cols], sq[:, cols], f32(sq_hi[:, cols]), ALU.subtract)\
                       .then_inc(sq_split, 1)

            unit(Unit(DF, DF_UNITS - 1), None)

            for c in range(sum(map(sum, LAST_PLAN["chunks"])), 8 * SB_UNITS):
                stage(None, c)

            dve.wait_ge(proj_read, 6 * UNITS + 2 * SB_UNITS)
            dve.sem_inc(z_done, 2)

            for p, v in enumerate(Z_ORDER):
                halves = [slice(n * HALF, (n + 1) * HALF) for n in range(2)]
                if v < SB_UNITS:
                    dve.wait_ge(o_loaded[p % 2], 16 * (p // 2 + 1))
                    for n, cols in enumerate(halves):
                        z_half(p, n, early_z[:, v, cols], z_silu, v * 2 + (n + 1))
                else:
                    for n, cols in enumerate(halves):
                        dve.wait_ge(rms_done, p * 2 + (n + 1))
                        dve.scalar_tensor_tensor(o_in[p % 2][:, cols], o_in[p % 2][:, cols], gain_head[:, 0:1],
                                                 rms[:, cols], ALU.mult, ALU.mult).then_inc(normed, 1)
                    if p < DF_UNITS - 1:
                        sq_lo_part(p + 1)
                    for n, cols in enumerate(halves):
                        dve.wait_ge(normed, p * 2 + (n + 1))
                        z_half(p, n, z_ps[p % 2][:, cols], proj_read, v * 2 + (6 * UNITS + n + 1))
                for n in range(2):
                    z_lo_part(p, n)
                if p == DF_UNITS - 1:
                    dve.sem_inc(y_read, 4)

            dve.sem_inc(merged_done, 2)
            def merge(m):
                for b in range(2):
                    for n in range(2):
                        q = 2 * b + n
                        cols = slice(n * HALF, (n + 1) * HALF)
                        dve.wait_ge(halves_done, m * 12 + (2 * (G_FIN0 + 4 + b) + n + 1))
                        if q == 0:
                            dve.wait_ge(gates_done, m * 4 + 8)
                        dst = merged[:, m, cols] if b == 0 else gate[:, q, :]
                        dve.tensor_tensor(dst, bank[:, 4 + q, :], gate[:, q, :], ALU.mult).then_inc(y_read, 1)
                for n in range(2):
                    cols = slice(n * HALF, (n + 1) * HALF)
                    dve.wait_ge(y_read, m * 4 + (n + 7))
                    dve.tensor_tensor(merged[:, m, cols], merged[:, m, cols], gate[:, 2 + n, :],
                                      ALU.add).then_inc(merged_done, 1)

            def merged_lo(k):
                dve.wait_ge(m_hi_done, k + 1)
                dve.tensor_tensor(hT_lo[:, k, :], merged[:, k, :], f32(hT_hi[:, k, :]), ALU.subtract)\
                   .then_inc(m_done, 1)

            with dve.Fori(0, KC - 1) as m:
                merge(m)
            for k in range(KC - 1):
                merged_lo(k)
            merge(KC - 1)
            merged_lo(KC - 1)
            dve.wait_ge(m_done, KC)
            for k in range(KC):
                dve.wait_ge(w_last_hi_done, k + 1)
                dve.tensor_tensor(w_last_lo[:, k, :], raw[:, (G_LAST0 + k) % RAW, :], f32(w_last_hi[k]),
                                  ALU.subtract).then_inc(w_last_ready, 1)
            for t in range(NT):
                if t < NT - 1:
                    dve.wait_ge(out_ps, t + 1)
                else:
                    dve.wait_ge(halves_done, 2 * G_LAST0)
                dve.tensor_copy(merged[:, t, 0:HALF], bank[:, t, :]).then_inc(y_saved, 1)
            dve.wait_ge(late_loaded, 16)
            for t in range(NT):
                dve.wait_ge(sq_half[0], t + 1)
                dve.tensor_tensor(merged[:, t, 0:HALF], merged[:, t, 0:HALF], post[:, 0:HALF], ALU.mult)\
                   .then_inc(y_post, 1)
            dve.wait_ge(sq_half[0], NT)
            dve.tensor_scalar(sumsq, sumsq, 1.0 / D, EPS, ALU.mult, ALU.add).then_inc(left_mean, 1)
            for t in range(NT):
                dve.wait_ge(y_std, t + 2)
                dve.reciprocal(rstd[:, t:t + 1], std[:, t:t + 1]).then_inc(rstd_done, 1)
                dve.wait_ge(rstd_done, NT + t + 1)
                dve.scalar_tensor_tensor(y_right[:, t % 2, :], bank[:, t, :], rstd[:, t:t + 1], post[:, HALF:],
                                         ALU.mult, ALU.mult).then_inc(y_scaled, 1)
                dve.wait_ge(xr_loaded[t], 16)
                dve.wait_ge(y_scaled, t + 1)
                dve.tensor_tensor(x_again[:, t, HALF:], x_again[:, t, HALF:], y_right[:, t % 2, :], ALU.add)\
                   .then_inc(fin_right, 1)
                dve.wait_ge(y_post, t + 1)
                dve.scalar_tensor_tensor(x_again[:, t, 0:HALF], merged[:, t, 0:HALF], rstd[:, t:t + 1],
                                         x_again[:, t, 0:HALF], ALU.mult, ALU.add).then_inc(fin_left, 1)


def granules(w_in, w_gate, w_sb, w_df, w_out):
    import numpy as np

    def columns(w, c):
        part = w[:, c:c + P].reshape(-1, 4, P, P)
        return part.transpose(0, 2, 1, 3).reshape(-1, P, HALF)

    def column(u, part):
        return (u // 4) * 2048 + part * 512 + (u % 4) * P

    g = [columns(w_in, column(u, part)) for u in range(UNITS) for part in range(3)]
    g += [columns(w_in, column(u, 3)) for u in range(UNITS)]
    for m in range(KC):
        g += [columns(w_gate, m * P), columns(w_gate, D + m * P), columns(w_sb, m * P), columns(w_df, m * P)]
    g += [w_out[k * P:(k + 1) * P, n * HALF:(n + 1) * HALF][None] for n in range(2) for k in range(KC)]
    return np.ascontiguousarray(np.concatenate(g, axis=0))


def kernel(x, norm_pre, norm_post, w_in, w_gate, b_gate, w_branch_sb, w_branch_df, w_out, lambda_q, lambda_k,
           df_head_norm):
    import numpy as np
    import concourse.bacc as bacc
    from concourse.bass_utils import run_bass_kernel_spmd

    a = {n: np.asarray(v) for n, v in dict(
        x=x, norm_pre=norm_pre, norm_post=norm_post, w_in=w_in, w_gate=w_gate, b_gate=b_gate, w_sb=w_branch_sb,
        w_df=w_branch_df, w_out=w_out, lambda_q=lambda_q, lambda_k=lambda_k, head_norm=df_head_norm).items()}
    cont = np.ascontiguousarray
    ins = {
        "x_rev": cont(a["x"][0, ::-1]),
        "w_all": granules(a["w_in"][0], a["w_gate"][0], a["w_sb"][0], a["w_df"][0], a["w_out"][0]),
        "norm_pre_t": cont(a["norm_pre"][0].reshape(KC, P).T),
        "norm_post_r": cont(a["norm_post"][0]),
        "b_gate_t": cont(a["b_gate"][0].reshape(2 * KC, P).T),
        "lambda_q_r": cont(a["lambda_q"][0]),
        "lambda_k_r": cont(a["lambda_k"][0]),
        "head_norm_t": cont(a["head_norm"][0].reshape(P, 1)),
    }
    nc = bacc.Bacc("TRN2", target_bir_lowering=False, num_devices=1)
    args = [nc.dram_tensor(n, v.shape, mybir.dt.from_np(v.dtype), kind="ExternalInput").ap() for n, v in ins.items()]
    out = nc.dram_tensor("out_rev", (S, D), F32, kind="ExternalOutput").ap()
    o_dram = nc.dram_tensor("o_scratch", (UNITS, P, S), F32, kind="Internal").ap()
    xx, w_all, npre, npost, bg, lq, lk, hn = args
    build(nc, xx, w_all, npre, npost, bg, lq, lk, hn, out, o_dram)
    r = run_bass_kernel_spmd(nc, [ins], core_ids=[0])
    return r.results[0]["out_rev"][::-1].reshape(1, S, D)
```
